# Optimizing a Trainium2 kernel written in Bass

```python
import jax, jax.numpy as jnp
from jax import lax
import numpy as np

D_MODEL = 2048
BATCH = 1
SEQ = 256
DEPTH = 1

D_FF = 5632
POOL_WINDOWS = (2, 4, 8, 16)
POOL_GROUPS = 4
POOL_GROUP_DIM = 256
POOL_WIDTH = POOL_GROUPS * POOL_GROUP_DIM
N_HEADS = 16
N_KV_GROUPS = 4
HEADS_PER_GROUP = N_HEADS // N_KV_GROUPS
HEAD_DIM = 128
Q_WIDTH = N_HEADS * HEAD_DIM
KV_WIDTH = N_KV_GROUPS * HEAD_DIM
CMP_BLOCK = 32
CMP_STRIDE = 16
CMP_HIDDEN = 256
SEL_BLOCK = 64
SEL_TOPK = 16
WINDOW = 512
NSA_Q_BLOCK = 64
N_NSA_BRANCHES = 3
FORCE_BONUS = 1000.0
IN_WIDTH = POOL_WIDTH + Q_WIDTH + 6 * KV_WIDTH + N_NSA_BRANCHES * N_HEADS + 2 * D_MODEL
RMS_EPS = 1e-6

kernel_name = 'hybrid_pool_nsa_macaron_block'

def rms_norm(x, g):
    xf = x.astype(jnp.float32)
    y = xf * lax.rsqrt(jnp.mean(xf * xf, axis=-1, keepdims=True) + RMS_EPS)
    return (y * g.astype(jnp.float32)).astype(x.dtype)

def swiglu(x, w_gate, w_up, w_down):
    return (jax.nn.silu(x @ w_gate) * (x @ w_up)) @ w_down

def masked_softmax(s, mask):
    s = jnp.where(mask, s.astype(jnp.float32), -jnp.inf)
    m = jnp.max(s, axis=-1, keepdims=True)
    m = jnp.where(jnp.isfinite(m), m, 0.0)
    p = jnp.exp(s - m)
    return p / jnp.maximum(jnp.sum(p, axis=-1, keepdims=True), 1e-30)

def pool_mixer(xp, pool_w, pool_scale):
    B, S, _ = xp.shape
    xf = xp.astype(jnp.float32)
    csum = jnp.concatenate([jnp.zeros((B, 1, POOL_WIDTH), jnp.float32), jnp.cumsum(xf, axis=1)], axis=1)
    t = jnp.arange(S)
    outs = []
    for gi, win in enumerate(POOL_WINDOWS):
        sl = slice(gi * POOL_GROUP_DIM, (gi + 1) * POOL_GROUP_DIM)
        cg = csum[..., sl]
        lo = jnp.maximum(t + 1 - win, 0)
        cnt = jnp.minimum(t + 1, win).astype(jnp.float32)
        outs.append((cg[:, 1:] - cg[:, lo]) / cnt[None, :, None] - xf[..., sl])
    pooled = jnp.stack(outs, axis=2).astype(xp.dtype)
    y = jnp.einsum('bsgc,gcd->bsgd', pooled, pool_w).reshape(B, S, POOL_WIDTH)
    return y * pool_scale

def compress_blocks(t, pe, w1, w2):
    B, S, G, Dh = t.shape
    n_sub = CMP_BLOCK // CMP_STRIDE
    n_chunk = S // CMP_STRIDE
    n_cmp = n_chunk - n_sub + 1
    c = t.reshape(B, n_chunk, CMP_STRIDE, G, Dh)
    blocks = jnp.concatenate([c[:, i:i + n_cmp] for i in range(n_sub)], axis=2)
    blocks = blocks + pe[None, None, :, None, :]
    flat = jnp.transpose(blocks, (0, 1, 3, 2, 4)).reshape(B, n_cmp, G, CMP_BLOCK * Dh)
    return jax.nn.silu(flat @ w1) @ w2

def nsa_mixer(q, kc, vc, ks, vs, kw, vw, gate_logits, pe_k, pe_v, k_w1, k_w2, v_w1, v_w2):
    B, S = q.shape[0], q.shape[1]
    G, HPG, DH = N_KV_GROUPS, HEADS_PER_GROUP, HEAD_DIM
    q = q.reshape(B, S, G, HPG, DH) * (DH ** -0.5)
    kc, vc, ks, vs, kw, vw = [a.reshape(B, S, G, DH) for a in (kc, vc, ks, vs, kw, vw)]
    gates = jax.nn.sigmoid(gate_logits.reshape(B, S, N_NSA_BRANCHES, G, HPG))

    k_cmp = compress_blocks(kc, pe_k, k_w1, k_w2)
    v_cmp = compress_blocks(vc, pe_v, v_w1, v_w2)
    n_cmp = k_cmp.shape[1]
    cmp_start = jnp.arange(n_cmp) * CMP_STRIDE
    cmp_end = cmp_start + CMP_BLOCK - 1

    n_blk = S // SEL_BLOCK
    n_sel = min(SEL_TOPK, n_blk)
    blk = jnp.arange(n_blk)
    sel_start = blk * SEL_BLOCK
    overlap = ((cmp_start[:, None] <= sel_start[None, :] + SEL_BLOCK - 1)
               & (cmp_end[:, None] >= sel_start[None, :])).astype(jnp.float32)
    ksb = jnp.transpose(ks.reshape(B, n_blk, SEL_BLOCK, G, DH), (0, 3, 1, 2, 4))
    vsb = jnp.transpose(vs.reshape(B, n_blk, SEL_BLOCK, G, DH), (0, 3, 1, 2, 4))
    b_idx = jnp.arange(B)[:, None, None, None]
    g_idx = jnp.arange(G)[None, None, :, None]

    kwp = jnp.pad(kw, ((0, 0), (WINDOW, 0), (0, 0), (0, 0)))
    vwp = jnp.pad(vw, ((0, 0), (WINDOW, 0), (0, 0), (0, 0)))

    def q_block(i):
        s0 = i * NSA_Q_BLOCK
        qb = lax.dynamic_slice_in_dim(q, s0, NSA_Q_BLOCK, axis=1)
        gb = lax.dynamic_slice_in_dim(gates, s0, NSA_Q_BLOCK, axis=1)
        t = s0 + jnp.arange(NSA_Q_BLOCK)

        s_c = jnp.einsum('bqghd,bngd->bqghn', qb, k_cmp)
        m_c = (cmp_end[None, :] <= t[:, None])[None, :, None, None, :]
        p_c = masked_softmax(s_c, m_c)
        o_c = jnp.einsum('bqghn,bngd->bqghd', p_c.astype(v_cmp.dtype), v_cmp)

        imp = jnp.einsum('bqghn,nm->bqgm', p_c, overlap)
        cur = t // SEL_BLOCK
        valid = sel_start[None, :] <= t[:, None]
        forced = (blk[None, :] == 0) | (blk[None, :] == cur[:, None]) | (blk[None, :] == cur[:, None] - 1)
        score = jnp.where(valid[None, :, None, :],
                          imp + jnp.where(forced, FORCE_BONUS, 0.0)[None, :, None, :], -FORCE_BONUS)
        top_v, top_i = lax.top_k(score, n_sel)
        sel_ok = top_v > -1.0
        k_g = ksb[b_idx, g_idx, top_i]
        v_g = vsb[b_idx, g_idx, top_i].reshape(B, NSA_Q_BLOCK, G, n_sel * SEL_BLOCK, DH)
        s_s = jnp.einsum('bqghd,bqgnld->bqghnl', qb, k_g).reshape(B, NSA_Q_BLOCK, G, HPG, n_sel * SEL_BLOCK)
        kpos = (top_i[..., None] * SEL_BLOCK + jnp.arange(SEL_BLOCK)).reshape(B, NSA_Q_BLOCK, G, n_sel * SEL_BLOCK)
        m_s = jnp.repeat(sel_ok, SEL_BLOCK, axis=-1) & (kpos <= t[None, :, None, None])
        p_s = masked_softmax(s_s, m_s[:, :, :, None, :])
        o_s = jnp.einsum('bqghk,bqgkd->bqghd', p_s.astype(v_g.dtype), v_g)

        k_w = lax.dynamic_slice_in_dim(kwp, s0, NSA_Q_BLOCK + WINDOW, axis=1)
        v_w = lax.dynamic_slice_in_dim(vwp, s0, NSA_Q_BLOCK + WINDOW, axis=1)
        kpos_w = s0 - WINDOW + jnp.arange(NSA_Q_BLOCK + WINDOW)
        m_w = ((kpos_w[None, :] <= t[:, None]) & (kpos_w[None, :] > t[:, None] - WINDOW)
               & (kpos_w[None, :] >= 0))[None, :, None, None, :]
        s_w = jnp.einsum('bqghd,bkgd->bqghk', qb, k_w)
        p_w = masked_softmax(s_w, m_w)
        o_w = jnp.einsum('bqghk,bkgd->bqghd', p_w.astype(v_w.dtype), v_w)

        return (gb[:, :, 0, :, :, None] * o_c + gb[:, :, 1, :, :, None] * o_s
                + gb[:, :, 2, :, :, None] * o_w)

    out = lax.map(q_block, jnp.arange(S // NSA_Q_BLOCK))
    return jnp.moveaxis(out, 0, 1).reshape(B, S, Q_WIDTH)

def setup_inputs(seed: int = 0) -> dict:
    key = jax.random.key(seed)
    k = jax.random.split(key, 23)
    L = DEPTH
    f32 = jnp.float32

    def w(kk, shape, fan_in):
        return jax.random.normal(kk, shape, f32) * (fan_in ** -0.5)

    def gain(kk, shape):
        return 1.0 + 0.02 * jax.random.normal(kk, shape, f32)

    return {
        'x': jax.random.normal(k[0], (BATCH, SEQ, D_MODEL), f32),
        'ffn1_norm': gain(k[1], (L, D_MODEL)),
        'ffn1_w_gate': w(k[2], (L, D_MODEL, D_FF), D_MODEL),
        'ffn1_w_up': w(k[3], (L, D_MODEL, D_FF), D_MODEL),
        'ffn1_w_down': w(k[4], (L, D_FF, D_MODEL), D_FF),
        'mix_norm': gain(k[5], (L, D_MODEL)),
        'w_in': w(k[6], (L, D_MODEL, IN_WIDTH), D_MODEL),
        'pool_w': w(k[7], (L, POOL_GROUPS, POOL_GROUP_DIM, POOL_GROUP_DIM), POOL_GROUP_DIM),
        'pool_scale': gain(k[8], (L, POOL_WIDTH)),
        'cmp_pe_k': 0.1 * jax.random.normal(k[9], (L, CMP_BLOCK, HEAD_DIM), f32),
        'cmp_pe_v': 0.1 * jax.random.normal(k[10], (L, CMP_BLOCK, HEAD_DIM), f32),
        'cmp_k_w1': w(k[11], (L, CMP_BLOCK * HEAD_DIM, CMP_HIDDEN), CMP_BLOCK * HEAD_DIM),
        'cmp_k_w2': w(k[12], (L, CMP_HIDDEN, HEAD_DIM), CMP_HIDDEN),
        'cmp_v_w1': w(k[13], (L, CMP_BLOCK * HEAD_DIM, CMP_HIDDEN), CMP_BLOCK * HEAD_DIM),
        'cmp_v_w2': w(k[14], (L, CMP_HIDDEN, HEAD_DIM), CMP_HIDDEN),
        'w_pool_up': w(k[15], (L, POOL_WIDTH, D_MODEL), POOL_WIDTH),
        'w_nsa_up': w(k[16], (L, Q_WIDTH, D_MODEL), Q_WIDTH),
        'w_out': w(k[17], (L, D_MODEL, D_MODEL), D_MODEL),
        'ffn2_norm': gain(k[18], (L, D_MODEL)),
        'ffn2_w_gate': w(k[19], (L, D_MODEL, D_FF), D_MODEL),
        'ffn2_w_up': w(k[20], (L, D_MODEL, D_FF), D_MODEL),
        'ffn2_w_down': w(k[21], (L, D_FF, D_MODEL), D_FF),
        'final_norm': gain(k[22], (D_MODEL,)),
    }

def reference(x, ffn1_norm, ffn1_w_gate, ffn1_w_up, ffn1_w_down, mix_norm, w_in, pool_w, pool_scale,
              cmp_pe_k, cmp_pe_v, cmp_k_w1, cmp_k_w2, cmp_v_w1, cmp_v_w2, w_pool_up, w_nsa_up, w_out,
              ffn2_norm, ffn2_w_gate, ffn2_w_up, ffn2_w_down, final_norm):
    splits = np.cumsum([POOL_WIDTH, Q_WIDTH] + [KV_WIDTH] * 6 + [N_NSA_BRANCHES * N_HEADS, D_MODEL])
    h = x
    for l in range(DEPTH):
        h = h + 0.5 * swiglu(rms_norm(h, ffn1_norm[l]), ffn1_w_gate[l], ffn1_w_up[l], ffn1_w_down[l])
        u = rms_norm(h, mix_norm[l])
        proj = u @ w_in[l]
        (xp, q, kc, vc, ks, vs, kw, vw, nsa_g, g_pool, g_nsa) = jnp.split(proj, splits, axis=-1)
        a = pool_mixer(xp, pool_w[l], pool_scale[l])
        b = nsa_mixer(q, kc, vc, ks, vs, kw, vw, nsa_g, cmp_pe_k[l], cmp_pe_v[l],
                      cmp_k_w1[l], cmp_k_w2[l], cmp_v_w1[l], cmp_v_w2[l])
        merged = jax.nn.sigmoid(g_pool) * (a @ w_pool_up[l]) + jax.nn.sigmoid(g_nsa) * (b @ w_nsa_up[l])
        h = h + merged @ w_out[l]
        h = h + 0.5 * swiglu(rms_norm(h, ffn2_norm[l]), ffn2_w_gate[l], ffn2_w_up[l], ffn2_w_down[l])
    return rms_norm(h, final_norm)


_drawn_inputs = setup_inputs


def setup_inputs(seed=0):
    import zlib

    import numpy as np

    out = dict(_drawn_inputs(seed))
    spreads = {}
    factors = {'ffn1_norm': 6.281,
     'mix_norm': 5.638,
     'pool_scale': 20.992,
     'cmp_pe_k': 111.962,
     'cmp_pe_v': 109.109,
     'ffn2_norm': 24.939,
     'final_norm': 22.712}
    for name, (base, spread) in spreads.items():
        noise = np.random.default_rng([zlib.crc32(name.encode()), seed]).standard_normal(out[name].shape)
        drawn = base * np.exp(spread * noise) if base else spread * noise
        out[name] = __import__('jax').numpy.asarray(drawn.astype(out[name].dtype))
    for name, factor in factors.items():
        out[name] = (out[name] * factor).astype(out[name].dtype)
    return out
```

```python
import numpy as np
import concourse.bass as bass
from concourse import mybir

F32 = mybir.dt.float32
F32R = mybir.dt.float32r
ALU = mybir.AluOpType
ACT = mybir.ActivationFunctionType
AX = mybir.AxisListType

P = 128
S = 256
HALVES = S // P
D = 2048
DT = D // P
FF = 5632
FT = FF // P
CH = 512
CT = CH // P
NFF = FF // CH
ND = D // CH
HEADS, GROUPS, HPG, DH = 16, 4, 4, 128
KV = GROUPS * DH
POOL_W = 1024
POOL_WINDOWS = (2, 4, 8, 16)
CMP_BLOCK, CMP_STRIDE, CMP_HIDDEN = 32, 16, 256
NCMP = S // CMP_STRIDE - 1
CB = GROUPS * NCMP
GATES = 48
EPS = 1e-6
NEG = -3.0e38
QSCALE = float(DH) ** -0.5

COL = {"p0": 0, "p1": CH, "q0": POOL_W, "q1": POOL_W + CH, "q2": POOL_W + 2 * CH, "q3": POOL_W + 3 * CH}
for _n, _name in enumerate(("kc", "vc", "ks", "vs", "kw", "vw")):
    COL[_name] = POOL_W + HEADS * DH + _n * KV
COL["gates"] = COL["vw"] + KV
COL_GP = COL["gates"] + GATES
COL_GN = COL_GP + D

PIECES = ["kc", "vc", "ks", "cmpk", "kw", "cmpv", "vs", "vw", "p0", "p1", "q0", "q1", "q2", "q3", "gates"]
START = {name: 4 * n for n, name in enumerate(PIECES)}

U_UP1 = 0
U_DOWN1 = U_UP1 + 8 * NFF
U_IN = U_DOWN1 + 12 * ND
U_ATT = U_IN + 4 * (len(PIECES) - 1) + 1
U_NSA = U_ATT + 6 * ND
U_OUT = U_NSA + 8 * ND
U_UP2 = U_OUT + 4 * ND
U_DOWN2 = U_UP2 + 8 * NFF
U_END = U_DOWN2 + 12 * ND
DOWN_KT = [4, 4, 3] * 4
DOWN_K0 = [sum(DOWN_KT[:j]) for j in range(12)]

USE = {}


def _number_uses():
    count = {"A": 0, "B": 0}

    def use(key, pair):
        count[pair] += 1
        USE[key] = (pair, count[pair])

    for c in range(NFF):
        use(("gate", 0, c), "B")
        use(("up", 0, c), "A")
    for n in range(ND):
        use(("down", 0, n), "BA"[n % 2])
    for n, name in enumerate(x for x in PIECES if not x.startswith("cmp")):
        use(("in", name), "BA"[n % 2])
    for n in range(ND):
        use(("gp", n), "A")
        use(("pu", n), "B")
    for n in range(ND):
        use(("gn", n), "A")
        use(("nu", n), "B")
    for n in range(ND):
        use(("wo", n), "AB"[n % 2])
    for c in range(NFF):
        use(("gate", 1, c), "A")
        use(("up", 1, c), "B")
    for n in range(ND):
        use(("down", 1, n), "AB"[n % 2])


_number_uses()

R_X, R_HID1, R_H1 = 0, ND, ND + NFF
R_IN = {name: R_H1 + ND + n for n, name in enumerate(("kc", "vc", "ks", "kw", "q0", "q1", "q2", "q3"))}
R_M = R_H1 + ND + 8
R_H2 = R_M + ND
R_HID2 = R_H2 + ND
PLAIN_ROUNDS = 8


def split_no(r):
    return r + 1 if r < R_M else r + 1 - PLAIN_ROUNDS


STEPS = 6 * GROUPS


def step_of(t):
    g, j = divmod(t, 6)
    return g, j // 3, j % 3


def keys_of(t):
    _, i, br = step_of(t)
    return NCMP if br == 0 else P * (i + 1)


def key_tiles(t):
    return -(-keys_of(t) // P)


def prob_rounds(t):
    return sum(key_tiles(x) for x in range(t))


C_ID, C_CAUSAL, C_CMP, C_ROW = 0, P, P + 2 * S, P + 2 * S + 2 * 16
C_END = C_ROW + 2
R_G1, R_GM, R_G2, R_PS, R_PEK, R_PEV = 0, DT, 2 * DT, 3 * DT, 3 * DT + 8, 3 * DT + 8 + CMP_BLOCK


def build_block(nc, a, out):
    def at(name, shape, dt, offset):
        return nc.alloc_sbuf_tensor_at(name, shape, dt, offset=offset)

    def up32(n):
        return -(-n // 32) * 32

    KB = 1024
    base = 1152
    h = at("h", [P, HALVES, D], F32, base)
    o_x = base + 16 * KB
    xT_hi = at("xT_hi", [P, DT, S], F32R, o_x)
    xT_lo = at("xT_lo", [P, DT, S], F32R, o_x + 16 * KB)
    o_w = o_x + 32 * KB
    w_raw = at("w_raw", [P, 4, 2048], F32, o_w)
    w_lo = at("w_lo", [P, 4, 2048], F32R, o_w)
    w_hi = at("w_hi", [P, 2, 2048], F32R, o_w + 32 * KB)
    o_r = o_w + 48 * KB
    hidT_hi = at("hidT_hi", [P, FT, S], F32R, o_r)
    hidT_lo = at("hidT_lo", [P, FT, S], F32R, o_r + 44 * KB)
    qT = at("qT", [P, HEADS, S], F32, o_r)
    ksT = at("ksT", [P, GROUPS, S], F32, o_r + 16 * KB)
    kwT = at("kwT", [P, GROUPS, S], F32, o_r + 20 * KB)
    vs = at("vs", [P, HALVES, KV], F32, o_r + 24 * KB)
    vw = at("vw", [P, HALVES, KV], F32, o_r + 28 * KB)
    bT_hi = at("bT_hi", [P, HEADS, S], F32R, o_r + 32 * KB)
    bT_lo = at("bT_lo", [P, HEADS, S], F32R, o_r + 48 * KB)
    band = at("band", [P, HALVES, 4, S], F32, o_r + 32 * KB)
    pooledT = at("pooledT", [P, 8, S], F32, o_r + 40 * KB)
    pool_w = at("pool_w_sb", [P, 4, 2, 256], F32, o_r + 48 * KB)
    xp = at("xp", [P, HALVES, POOL_W], F32, o_r + 56 * KB)
    kcT = at("kcT", [P, GROUPS, S], F32, o_r + 64 * KB)
    vcT = at("vcT", [P, GROUPS, S], F32, o_r + 68 * KB)
    FLAT = CMP_BLOCK * CB + P - CB
    flat_raw = at("flat_raw", [P, FLAT], F32, o_r + 72 * KB)
    flat_lo = at("flat_lo", [P, FLAT], F32R, o_r + 72 * KB)
    flat_hi = at("flat_hi", [P, FLAT], F32R, o_r + 80 * KB)
    aT_hi = at("aT_hi", [P, 8, S], F32R, o_r + 64 * KB)
    aT_lo = at("aT_lo", [P, 8, S], F32R, o_r + 72 * KB)
    prob = at("prob", [P, 2, HPG, S], F32, o_r + 80 * KB)
    mT_hi = at("mT_hi", [P, DT, S], F32R, o_r)
    mT_lo = at("mT_lo", [P, DT, S], F32R, o_r + 16 * KB)
    o_m = o_r + 88 * KB
    merged = at("merged", [P, HALVES, D], F32, o_m)
    small = at("small", [P, P], F32, o_m)
    cmp_h = at("cmp_h", [P, CMP_HIDDEN], F32, o_m + 1 * KB)
    cmp_hT = at("cmp_hT", [P, 2, P], F32, o_m + 2 * KB)
    cmp_w2 = at("cmp_w2", [P, 2, 2, DH], F32, o_m + 3 * KB)
    o_p = o_m + 16 * KB
    probT = at("probT", [P, 2, 2, CH], F32, o_p)
    gain_last = at("gain_last", [P, D], F32, o_p)
    tok = at("tok", [P, HALVES, CH], F32, o_p + 8 * KB)
    head_out = at("head_out", [P, 2, CH], F32, o_p + 8 * KB)
    gate = at("gate", [P, HALVES, CH], F32, o_p + 12 * KB)
    o_c = o_p + 16 * KB
    const = at("const", [P, C_END], F32, o_c)
    o_t = o_c + up32(4 * C_END)
    small_T = at("small_T", [P, P], F32, o_t)
    o_s = o_t + 4 * P
    kcmpT = at("kcmpT", [P, CB], F32, o_s)
    vcmp = at("vcmp", [P, GROUPS, DH], F32, o_s + up32(4 * CB))
    o_s += up32(4 * CB) + 4 * KV
    bgate = at("bgate", [P, HALVES, GATES], F32, o_s)
    o_s += 4 * HALVES * GATES
    sumsq = at("sumsq", [P, HALVES, ND], F32, o_s)
    var = at("var", [P, HALVES], F32, o_s + 32)
    std = at("std", [P, HALVES], F32, o_s + 64)
    rstd = at("rstd", [P, HALVES], F32, o_s + 96)
    qstd = at("qstd", [P, HALVES], F32, o_s + 128)
    top = at("top", [P, 2, HPG], F32, o_s + 160)
    ntop = at("ntop", [P, 2, HPG], F32, o_s + 192)
    psums = at("psums", [P, 3, HPG], F32, o_s + 224)
    coef = at("coef", [P, 3, HPG], F32, o_s + 288)

    ps = nc.alloc_psum_tensor("ps", [P, 8 * CH], F32)

    def bank(b, n=1):
        return ps[:, b * CH:(b + n) * CH]

    ACC = {"A": bank(0, 2).rearrange("p (h n) -> p h n", h=2),
           "B": bank(2, 2).rearrange("p (h n) -> p h n", h=2)}
    T45 = bank(4, 2).rearrange("p (f s) -> p f s", f=CT)
    T67 = bank(6, 2).rearrange("p (f s) -> p f s", f=CT)
    SCORES = bank(6, 2).rearrange("p (h k) -> p h k", h=HPG)
    PT = bank(4)
    HO = bank(5)
    CMP = bank(6)
    CMP2 = bank(7)

    def T_of(r):
        return T67 if r < ND and r % 2 else T45

    ident = const[:, C_ID:C_ID + P]
    causal = const[:, C_CAUSAL:C_CAUSAL + 2 * S].rearrange("p (i k) -> p i k", i=2)
    cmask = const[:, C_CMP:C_CMP + 32].rearrange("p (i k) -> p i k", i=2)
    rowok = const[:, C_ROW:C_ROW + 2]

    def sem(name):
        return nc.alloc_semaphore(name)

    raw_loaded = [sem(f"raw_loaded{n}") for n in range(4)]
    x_loaded = [sem(f"x_loaded{n}") for n in range(ND)]
    small_loaded = sem("small_loaded")
    const_loaded = sem("const_loaded")
    pool_loaded = sem("pool_loaded")
    gain_loaded = sem("gain_loaded")
    out_stored = sem("out_stored")
    hi_ready = sem("hi_ready")
    unit_split = sem("unit_split")
    unit_used = sem("unit_used")
    pair_read = {p: sem(f"pair_read_{p}") for p in "AB"}
    t_done = sem("t_done")
    t_hi = sem("t_hi")
    t_read = sem("t_read")
    small_cleared = sem("small_cleared")
    small_t = sem("small_t")
    small_ready = sem("small_ready")
    sumsq_ready = sem("sumsq_ready")
    var_ready = sem("var_ready")
    std_ready = sem("std_ready")
    rstd_ready = sem("rstd_ready")
    flat_raw_ready = sem("flat_raw_ready")
    flat_hi_ready = sem("flat_hi_ready")
    flat_ready = sem("flat_ready")
    cmp_act = sem("cmp_act")
    cmp_mm = sem("cmp_mm")
    cmp_copied = sem("cmp_copied")
    pool_mm = sem("pool_mm")
    pool_hi = sem("pool_hi")
    pool_read = sem("pool_read")
    scores_done = sem("scores_done")
    masked = sem("masked")
    probs_done = sem("probs_done")
    pt_done = sem("pt_done")
    pt_copied = sem("pt_copied")
    heads_done = sem("heads_done")
    heads_read = sem("heads_read")
    b_t = sem("b_t")
    b_hi = sem("b_hi")
    b_read = sem("b_read")
    dve_step = sem("dve_step")

    def by(value, step, i):
        return value if i is None else i * step + value

    def cols(s, q, n):
        def view(x):
            return x[:, 0:q * n].rearrange("p (q n) -> p q n", q=q)
        return view(w_raw[:, s % 4, :]), view(w_hi[:, s % 2, :]), view(w_lo[:, s % 4, :])

    SHAPE = {}
    for s in range(U_END):
        SHAPE[s] = (4, CH)
    for first in (U_DOWN1, U_DOWN2):
        for n in range(ND):
            for j in range(12):
                SHAPE[first + 12 * n + j] = (DOWN_KT[j], CH)
    for name in ("cmpk", "cmpv"):
        for j in range(4):
            SHAPE[U_IN + START[name] + j] = (8, CMP_HIDDEN)
    SHAPE[U_IN + START["gates"]] = (DT, GATES)

    FFNS = [(0, U_UP1, U_DOWN1, R_HID1), (1, U_UP2, U_DOWN2, R_HID2)]

    with nc.Block() as block:

        @block.sync
        def _(sp):
            def load(s, src, i=None):
                if s >= 4:
                    sp.wait_ge(unit_used, by(s - 3, 8, i))
                q, n = SHAPE[s]
                sp.dma_start(cols(s, q, n)[0], src).then_inc(raw_loaded[s % 4], 16)

            def rows(w, k0, q, n0, n=CH):
                return w[k0 * P:(k0 + q) * P, n0:n0 + n].rearrange("(q p) n -> p q n", p=P)

            def gate_up(first, wg, wu, i=None):
                for j in range(8):
                    w = wg if j < 4 else wu
                    k = w[(j % 4) * CH:(j % 4 + 1) * CH, :].rearrange("(q p) n -> p q n", p=P)
                    src = k[:, :, 0:CH] if i is None else k[:, :, bass.ds((i + 1) * CH, CH)]
                    load(first + j, src, i)

            def ffn(k, wg, wu, wd):
                _, up, down, _ = FFNS[k]
                if k == 1:
                    gate_up(up, wg, wu)
                with sp.Fori(0, NFF - 1) as i:
                    gate_up(up + 8, wg, wu, i)
                for n in range(ND):
                    for j in range(12):
                        load(down + 12 * n + j, rows(wd, DOWN_K0[j], DOWN_KT[j], n * CH))

            xv = a["x"].rearrange("(i p) d -> p i d", p=P)

            def load_x(n):
                sp.dma_start(h[:, :, n * CH:(n + 1) * CH], xv[:, :, n * CH:(n + 1) * CH]).then_inc(x_loaded[n], 16)

            load_x(0)
            sp.dma_start(const[:, :], a["shape_consts"]).then_inc(const_loaded, 16)
            sp.wait_ge(small_cleared, 1)
            for r, name, m in ((R_G1, "ffn1_norm", DT), (R_GM, "mix_norm", DT), (R_G2, "ffn2_norm", DT),
                               (R_PS, "pool_scale", 8)):
                sp.dma_start(small[r:r + m, :], a[name].rearrange("(r c) -> r c", c=P)).then_inc(small_loaded, 16)
            sp.dma_start(small[R_PEK:R_PEK + CMP_BLOCK, :], a["cmp_pe_k"]).then_inc(small_loaded, 16)
            sp.dma_start(small[R_PEV:R_PEV + CMP_BLOCK, :], a["cmp_pe_v"]).then_inc(small_loaded, 16)
            wg, wu = a["ffn1_w_gate"], a["ffn1_w_up"]
            for j in range(4):
                load(j, rows(wg, 4 * j, 4, 0))
                if j < 3:
                    load_x(j + 1)
            for n, name in enumerate(("cmp_k_w2", "cmp_v_w2")):
                sp.dma_start(cmp_w2[:, n, :, :], a[name].rearrange("(q p) d -> p q d", p=P)).then_inc(small_loaded, 16)
            for j in range(4):
                load(4 + j, rows(wu, 4 * j, 4, 0))
            ffn(0, wg, wu, a["ffn1_w_down"])

            for name in PIECES:
                s = U_IN + START[name]
                if name.startswith("cmp"):
                    w1 = a["cmp_k_w1"] if name == "cmpk" else a["cmp_v_w1"]
                    for j in range(4):
                        load(s + j, rows(w1, 8 * j, 8, 0, CMP_HIDDEN))
                elif name == "gates":
                    load(s, rows(a["w_in"], 0, DT, COL["gates"], GATES))
                else:
                    for j in range(4):
                        load(s + j, rows(a["w_in"], 4 * j, 4, COL[name]))
                if name == "vc":
                    sp.dma_start(band[:, :, :, :], a["pool_band"]).then_inc(pool_loaded, 16)
                    sp.dma_start(pool_w[:, :, :, :],
                                 a["pool_w"].rearrange("g (q p) d -> p g q d", p=P)).then_inc(pool_loaded, 16)
            for n in range(ND):
                for j in range(4):
                    load(U_ATT + 6 * n + j, rows(a["w_in"], 4 * j, 4, COL_GP + n * CH))
                for j in range(2):
                    load(U_ATT + 6 * n + 4 + j, rows(a["w_pool_up"], 4 * j, 4, n * CH))
            for n in range(ND):
                for j in range(4):
                    load(U_NSA + 8 * n + j, rows(a["w_in"], 4 * j, 4, COL_GN + n * CH))
                for j in range(4):
                    load(U_NSA + 8 * n + 4 + j, rows(a["w_nsa_up"], 4 * j, 4, n * CH))
            for n in range(ND):
                for j in range(4):
                    load(U_OUT + 4 * n + j, rows(a["w_out"], 4 * j, 4, n * CH))
            sp.dma_start(gain_last[:, :], a["final_norm"].partition_broadcast(P)).then_inc(gain_loaded, 16)
            ffn(1, a["ffn2_w_gate"], a["ffn2_w_up"], a["ffn2_w_down"])
            sp.wait_ge(out_stored, 32)

        @block.scalar
        def _(act):
            def hi(s, i=None):
                if s >= U_END:
                    return
                q, n = SHAPE[s]
                act.wait_ge(raw_loaded[s % 4], by(16 * (s // 4 + 1), 32, i))
                if s >= 2:
                    act.wait_ge(unit_used, by(s - 1, 8, i))
                act.activation(w_hi[:, s % 2, 0:q * n], w_raw[:, s % 4, 0:q * n], ACT.Copy).then_inc(hi_ready, 1)

            def wait_read(key, i=None):
                p, n = USE[key]
                act.wait_ge(pair_read[p], by(n, 1, i))

            def evacuate(key, last_unit, dst, func, scale, i=None, width=CH):
                p, _ = USE[key]
                act.wait_ge(unit_used, by(last_unit + 1, 8, i))
                act.activation(dst(0), ACC[p][:, 0, 0:width], func, scale=scale[:, 0:1])
                act.activation(dst(1), ACC[p][:, 1, 0:width], func, scale=scale[:, 1:2]).then_inc(pair_read[p], 1)

            def turned_hi(r, dst, i=None):
                act.wait_ge(t_done, by(r + 1, 1, i))
                act.activation(dst, T_of(r), ACT.Copy).then_inc(t_hi, 1)

            def turned_hi_gain(r, dst, n, g0):
                act.wait_ge(t_done, r + 1)
                for f in range(CT):
                    c = g0 + CT * n + f
                    op = act.activation(dst[:, CT * n + f, :], T_of(r)[:, f, :], ACT.Copy, scale=small_T[:, c:c + 1])
                op.then_inc(t_hi, 1)

            squared = [0]

            def squares(n):
                if squared[0]:
                    act.wait_ge(sumsq_ready, squared[0])
                squared[0] += 1
                for k in range(HALVES):
                    op = act.activation(gate[:, k, :], h[:, k, n * CH:(n + 1) * CH], ACT.Square,
                                        accum_out=sumsq[:, k, n:n + 1])
                op.then_inc(sumsq_ready, 1)

            def root(k):
                act.wait_ge(var_ready, k + 1)
                act.activation(std[:, :], var[:, :], ACT.Sqrt).then_inc(std_ready, 1)

            def silu(k, first, i=None):
                key = ("gate", k, 0 if i is None else 1)
                up = ("up", k, 0 if i is None else 1)
                p, n = USE[up]
                if n > 1:
                    act.wait_ge(pair_read[p], by(n - 1, 1, i))
                evacuate(key, first + 3, lambda m: gate[:, m, :], ACT.Silu, rstd, i)

            def ffn(k, tail):
                _, up, down, r0 = FFNS[k]
                for j in range(8):
                    hi(up + j + 1)
                    tail(j)
                    if j == 4:
                        act.wait_ge(rstd_ready, 1 if k == 0 else 3)
                        silu(k, up)
                with act.Fori(0, NFF - 1) as i:
                    for j in range(8):
                        hi(up + 8 + j + 1, i)
                        if j == 2:
                            turned_hi(r0, hidT_hi[:, bass.ds(i * CT, CT), :], i)
                        if j == 4:
                            silu(k, up + 8, i)
                for n in range(ND):
                    for j in range(12):
                        hi(down + 12 * n + j + 1)
                        if n:
                            down_tail(k, n - 1, j)
                        elif j == 2:
                            turned_hi(r0 + NFF - 1, hidT_hi[:, FT - CT:FT, :])

            def down_tail(k, n, j):
                if j == 1:
                    wait_read(("down", k, n))
                    squares(n)
                if j == 2 and k == 0:
                    turned_hi_gain(R_H1 + n, xT_hi, n, R_GM)

            hi(0)
            act.wait_ge(small_ready, 1)
            for n in range(ND):
                turned_hi_gain(R_X + n, xT_hi, n, R_G1)
                act.wait_ge(x_loaded[n], 16)
                squares(n)
            root(0)

            ffn(0, lambda j: None)

            outs = {"kc": tok, "vc": tok, "ks": tok, "kw": tok, "vs": vs, "vw": vw, "p0": xp, "p1": xp,
                    "q0": tok, "q1": tok, "q2": tok, "q3": tok}
            for m, name in enumerate(PIECES):
                last = PIECES[m - 1] if m else None
                for j in range(1 if name == "gates" else 4):
                    u = START[name] + j
                    hi(U_IN + u + 1)
                    if m == 0:
                        down_tail(0, ND - 1, j)
                        if j == 2:
                            root(1)
                    elif j == 0 and not last.startswith("cmp"):
                        if m == 1:
                            act.wait_ge(rstd_ready, 2)
                        dst = outs[last]
                        if dst is tok:
                            act.wait_ge(t_done, R_IN[last])
                        n0 = CH if last == "p1" else 0
                        evacuate(("in", last), U_IN + u - 1, lambda k: dst[:, k, n0:n0 + CH],
                                 ACT.Copy, qstd if last[0] == "q" else rstd)
                    if u in (START["ks"] + 1, START["kw"] + 1):
                        k = int(u > START["kw"])
                        act.wait_ge(flat_raw_ready, k + 1)
                        act.activation(flat_hi[:, :], flat_raw[:, :], ACT.Copy).then_inc(flat_hi_ready, 1)
                    if u in (START["cmpk"] + 4, START["cmpv"] + 4):
                        k = int(u > START["cmpk"] + 4)
                        act.wait_ge(unit_used, U_IN + u)
                        act.activation(cmp_h[:, :], CMP[:, 0:CMP_HIDDEN], ACT.Silu).then_inc(cmp_act, 1)
                    if u in (START["p1"] + 11, START["p1"] + 13):
                        b = (u - START["p1"] - 11) // 2
                        act.wait_ge(pool_mm, b + 3)
                        for f in range(CT):
                            c = R_PS + 4 * b + f
                            op = act.activation(aT_hi[:, 4 * b + f, :], T67[:, f, :], ACT.Copy,
                                                scale=small_T[:, c:c + 1])
                        op.then_inc(pool_hi, 1)

            def attention(t):
                def copy_turned(x, kb):
                    r = prob_rounds(x) + kb
                    act.wait_ge(pt_done, r + 1)
                    if x >= 2:
                        act.wait_ge(heads_done, x - 1)
                    m = NCMP if keys_of(x) == NCMP else P
                    act.activation(probT[0:m, x % 2, kb, :], PT[0:m, :], ACT.Copy).then_inc(pt_copied, 1)

                if 1 <= t <= STEPS:
                    copy_turned(t - 1, 0)
                if t >= 6 and t % 3 == 0:
                    x = t // 3 - 2
                    act.wait_ge(b_t, x + 1)
                    act.activation(bT_hi[:, HPG * (x // 2):HPG * (x // 2 + 1), (x % 2) * P:(x % 2 + 1) * P],
                                   HO.rearrange("p (f s) -> p f s", f=HPG), ACT.Copy).then_inc(b_hi, 1)
                if t < STEPS:
                    nk = keys_of(t)
                    act.wait_ge(masked, t + 1)
                    if t >= 3:
                        act.wait_ge(heads_read, t - 2)
                    for k in range(HPG):
                        op = act.activation(prob[:, t % 2, k, 0:nk], prob[:, t % 2, k, 0:nk], ACT.Exp,
                                            bias=ntop[:, t % 2, k:k + 1], accum_out=psums[:, t % 3, k:k + 1])
                    op.then_inc(probs_done, 1)
                if 1 <= t <= STEPS and key_tiles(t - 1) == 2:
                    copy_turned(t - 1, 1)

            for n in range(ND):
                for j in range(6):
                    u = U_ATT + 6 * n + j
                    hi(u + 1)
                    if n == 0 and j == 0:
                        evacuate(("in", "gates"), u - 1, lambda k: bgate[:, k, :], ACT.Sigmoid, rstd, width=GATES)
                    if j == 4:
                        if n:
                            wait_read(("pu", n - 1))
                        evacuate(("gp", n), u - 1, lambda k: gate[:, k, :], ACT.Sigmoid, rstd)
                    attention(u - U_ATT)
            for n in range(ND):
                for j in range(8):
                    u = U_NSA + 8 * n + j
                    hi(u + 1)
                    if n == 0 and j < 4:
                        attention(STEPS + j)
                    if j == 2 and n:
                        turned_hi(R_M + n - 1, mT_hi[:, CT * (n - 1):CT * n, :])
                    if j == 4:
                        wait_read(("nu", n - 1) if n else ("pu", ND - 1))
                        evacuate(("gn", n), u - 1, lambda k: gate[:, k, :], ACT.Sigmoid, rstd)

            def out_tail(n, j):
                if j == 1:
                    wait_read(("wo", n))
                    squares(n)
                if j == 2:
                    turned_hi_gain(R_H2 + n, xT_hi, n, R_G2)
                    if n == ND - 1:
                        root(2)

            for n in range(ND):
                for j in range(4):
                    hi(U_OUT + 4 * n + j + 1)
                    if n:
                        out_tail(n - 1, j)
                    elif j == 2:
                        turned_hi(R_M + ND - 1, mT_hi[:, DT - CT:DT, :])
            ffn(1, lambda j: out_tail(ND - 1, j))
            wait_read(("down", 1, ND - 1))
            squares(ND - 1)
            root(3)
            act.wait_ge(rstd_ready, 4)
            act.activation(h[:, 1, :], h[:, 1, :], ACT.Copy, scale=rstd[:, 1:2]).then_inc(hi_ready, 1)
            act.wait_ge(hi_ready, U_END + 1)
            ov = out.rearrange("(i p) d -> p i d", p=P)
            act.dma_start(ov[:, 1, :], h[:, 1, :]).then_inc(out_stored, 16)
            act.wait_ge(unit_split, U_END + 1)
            act.dma_start(ov[:, 0, :], h[:, 0, :]).then_inc(out_stored, 16)

        @block.vector
        def _(dve):
            steps = [0]

            def chain(op):
                steps[0] += 1
                op.then_inc(dve_step, 1)
                dve.wait_ge(dve_step, steps[0])

            def lo(s, i=None):
                if s >= U_END:
                    return
                q, n = SHAPE[s]
                dve.wait_ge(hi_ready, by(s + 1, 8, i))
                dve.tensor_tensor(w_lo[:, s % 4, 0:q * n], w_raw[:, s % 4, 0:q * n],
                                  w_hi[:, s % 2, 0:q * n].bitcast(F32), ALU.subtract).then_inc(unit_split, 1)

            def turned_lo(r, dst_lo, dst_hi, i=None):
                dve.wait_ge(t_hi, by(split_no(r), 1, i))
                dve.tensor_tensor(dst_lo, T_of(r), dst_hi.bitcast(F32), ALU.subtract).then_inc(t_read, 1)

            def turned_lo_gain(r, n, g0):
                dve.wait_ge(t_hi, split_no(r))
                for f in range(CT):
                    c, x = g0 + CT * n + f, CT * n + f
                    op = dve.scalar_tensor_tensor(out=xT_lo[:, x, :], in0=T_of(r)[:, f, :],
                                                  scalar=small_T[:, c:c + 1], in1=xT_hi[:, x, :].bitcast(F32),
                                                  op0=ALU.mult, op1=ALU.subtract)
                op.then_inc(t_read, 1)

            def turned_plain(r, dst):
                dve.wait_ge(t_done, r + 1)
                dve.tensor_copy(dst, T_of(r)).then_inc(t_read, 1)

            def rstd_of(k):
                dve.wait_ge(sumsq_ready, ND * (k + 1))
                chain(dve.tensor_reduce(out=var[:, :], in_=sumsq[:, :, :], axis=AX.X, op=ALU.add))
                dve.tensor_scalar(var[:, :], var[:, :], 1.0 / D, EPS, ALU.mult, ALU.add).then_inc(var_ready, 1)

            def rstd_end(k):
                dve.wait_ge(std_ready, k + 1)
                if k == 1:
                    chain(dve.reciprocal(rstd[:, :], std[:, :]))
                    dve.tensor_scalar(qstd[:, :], rstd[:, :], QSCALE, None, ALU.mult).then_inc(rstd_ready, 1)
                else:
                    dve.reciprocal(rstd[:, :], std[:, :]).then_inc(rstd_ready, 1)

            def residual(key, last_unit, n, factor):
                p, _ = USE[key]
                dve.wait_ge(unit_used, last_unit + 1)
                for k in range(HALVES):
                    x = h[:, k, n * CH:(n + 1) * CH]
                    op = dve.scalar_tensor_tensor(out=x, in0=ACC[p][:, k, :], scalar=factor, in1=x,
                                                  op0=ALU.mult, op1=ALU.add)
                op.then_inc(pair_read[p], 1)

            def hidden(k, first, i=None):
                key = 0 if i is None else 1
                dve.wait_ge(pair_read[USE["gate", k, key][0]], by(USE["gate", k, key][1], 1, i))
                dve.wait_ge(unit_used, by(first + 8, 8, i))
                dve.wait_ge(t_done, by(FFNS[k][3] + key, 1, i))
                p, _ = USE["up", k, key]
                for m in range(HALVES):
                    op = dve.scalar_tensor_tensor(out=tok[:, m, :], in0=ACC[p][:, m, :], scalar=rstd[:, m:m + 1],
                                                  in1=gate[:, m, :], op0=ALU.mult, op1=ALU.mult)
                op.then_inc(pair_read[p], 1)

            def hidden_of_loop(k, first, i):
                dve.wait_ge(pair_read[USE["gate", k, 0][0]], by(USE["gate", k, 0][1], 1, i))
                dve.wait_ge(unit_used, by(first, 8, i))
                dve.wait_ge(t_done, by(FFNS[k][3], 1, i))
                p, _ = USE["up", k, 0]
                for m in range(HALVES):
                    op = dve.scalar_tensor_tensor(out=tok[:, m, :], in0=ACC[p][:, m, :], scalar=rstd[:, m:m + 1],
                                                  in1=gate[:, m, :], op0=ALU.mult, op1=ALU.mult)
                op.then_inc(pair_read[p], 1)

            def ffn(k, tail):
                _, up, down, r0 = FFNS[k]
                for j in range(8):
                    lo(up + j + 1)
                    tail(j)
                with dve.Fori(0, NFF - 1) as i:
                    for j in range(8):
                        lo(up + 8 + j + 1, i)
                        if j == 0:
                            hidden_of_loop(k, up + 8, i)
                        if j == 2:
                            d = bass.ds(i * CT, CT)
                            turned_lo(r0, hidT_lo[:, d, :], hidT_hi[:, d, :], i)
                for n in range(ND):
                    for j in range(12):
                        lo(down + 12 * n + j + 1)
                        if n:
                            down_tail(k, n - 1, j)
                            continue
                        if j == 0:
                            c = NFF - 1
                            dve.wait_ge(pair_read[USE["gate", k, c][0]], USE["gate", k, c][1])
                            dve.wait_ge(unit_used, down)
                            dve.wait_ge(t_done, r0 + c)
                            p, _ = USE["up", k, c]
                            for m in range(HALVES):
                                op = dve.scalar_tensor_tensor(out=tok[:, m, :], in0=ACC[p][:, m, :],
                                                              scalar=rstd[:, m:m + 1], in1=gate[:, m, :],
                                                              op0=ALU.mult, op1=ALU.mult)
                            op.then_inc(pair_read[p], 1)
                        if j == 2:
                            turned_lo(r0 + NFF - 1, hidT_lo[:, FT - CT:FT, :], hidT_hi[:, FT - CT:FT, :])

            def gain_out(n):
                dve.wait_ge(sumsq_ready, 3 * ND + n + 1)
                for k in range(HALVES):
                    x = h[:, k, n * CH:(n + 1) * CH]
                    op = dve.tensor_tensor(x, x, gain_last[:, n * CH:(n + 1) * CH], ALU.mult)
                return op

            def down_tail(k, n, j):
                if j == 0:
                    residual(("down", k, n), FFNS[k][2] + 12 * n + 11, n, 0.5)
                if j == 2 and k == 0:
                    turned_lo_gain(R_H1 + n, n, R_GM)
                if j == 11 and k == 1:
                    dve.wait_ge(gain_loaded, 16)
                    gain_out(n)

            dve.memset(small[:, :], 0.0).then_inc(small_cleared, 1)
            dve.wait_ge(small_t, 1)
            dve.tensor_copy(small_T[:, :], CMP2[:, 0:P]).then_inc(small_ready, 1)
            dve.wait_ge(small_ready, 1)
            lo(0)
            for n in range(ND):
                turned_lo_gain(R_X + n, n, R_G1)
            rstd_of(0)
            rstd_end(0)

            ffn(0, lambda j: None)

            turned = {"kc": kcT, "vc": vcT, "ks": ksT, "kw": kwT}
            for m, name in enumerate(PIECES):
                for j in range(1 if name == "gates" else 4):
                    u = START[name] + j
                    lo(U_IN + u + 1)
                    if m == 0:
                        down_tail(0, ND - 1, j)
                        if j == 1:
                            rstd_of(1)
                        if j == 2:
                            rstd_end(1)
                    if m and j == 2:
                        last = PIECES[m - 1]
                        if last in turned:
                            turned_plain(R_IN[last], turned[last][:, :, :])
                        elif last[0] == "q":
                            g = int(last[1])
                            turned_plain(R_IN[last], qT[:, HPG * g:HPG * (g + 1), :])
                    if u in (START["ks"], START["cmpk"] + 4):
                        k = int(u > START["ks"])
                        if k:
                            dve.wait_ge(unit_used, U_IN + START["cmpk"] + 4)
                        dve.memset(flat_raw[:, CMP_BLOCK * CB:FLAT], 0.0)
                        src = (vcT if k else kcT)[:, :, :].rearrange("p g (c r) -> p r g c", r=CMP_STRIDE)
                        dst = flat_raw[:, 0:CMP_BLOCK * CB].rearrange("p (j g n) -> p j g n", j=CMP_BLOCK, g=GROUPS)
                        pe0 = R_PEV if k else R_PEK
                        dve.wait_ge(t_read, R_IN["vc" if k else "kc"] + 1)
                        for s in range(2):
                            for g in range(GROUPS):
                                pe = small_T[:, pe0 + 16 * s:pe0 + 16 * (s + 1)].unsqueeze(2)
                                op = dve.tensor_tensor(dst[:, 16 * s:16 * (s + 1), g, :], src[:, :, g, s:s + NCMP],
                                                       pe.to_broadcast([P, 16, NCMP]), ALU.add)
                        op.then_inc(flat_raw_ready, 1)
                    if u in (START["ks"] + 2, START["kw"] + 2):
                        k = int(u > START["kw"])
                        dve.wait_ge(flat_hi_ready, k + 1)
                        dve.tensor_tensor(flat_lo[:, :], flat_raw[:, :], flat_hi[:, :].bitcast(F32),
                                          ALU.subtract).then_inc(flat_ready, 1)
                    if u in (START["cmpk"] + 6, START["cmpv"] + 6):
                        k = int(u > START["cmpk"] + 6)
                        dve.wait_ge(cmp_mm, 2 * k + 1)
                        dve.tensor_copy(cmp_hT[:, :, :], CMP2[:, 0:2 * P].rearrange("p (q n) -> p q n", q=2))\
                           .then_inc(cmp_copied, 1)
                        dve.wait_ge(cmp_mm, 2 * k + 2)
                        if k:
                            dve.tensor_copy(vcmp[0:NCMP, :, :], CMP[0:NCMP, :].rearrange("p (g d) -> p g d", g=GROUPS))\
                               .then_inc(cmp_copied, 1)
                        else:
                            dve.tensor_copy(kcmpT[:, :], CMP[:, 0:CB]).then_inc(cmp_copied, 1)
                    if u in (START["p1"] + 7, START["p1"] + 9):
                        b = (u - START["p1"] - 7) // 2
                        dve.wait_ge(pool_mm, b + 1)
                        dve.tensor_copy(pooledT[:, 4 * b:4 * b + 4, :], T67).then_inc(pool_read, 1)
                    if u in (START["p1"] + 11, START["p1"] + 13):
                        b = (u - START["p1"] - 11) // 2
                        dve.wait_ge(pool_hi, b + 1)
                        for f in range(CT):
                            c, x = R_PS + 4 * b + f, 4 * b + f
                            op = dve.scalar_tensor_tensor(out=aT_lo[:, x, :], in0=T67[:, f, :],
                                                          scalar=small_T[:, c:c + 1], in1=aT_hi[:, x, :].bitcast(F32),
                                                          op0=ALU.mult, op1=ALU.subtract)
                        op.then_inc(pool_read, 1)

            def attention(t):
                if t < STEPS:
                    g, i, br = step_of(t)
                    nk = keys_of(t)
                    dve.wait_ge(scores_done, t + 1)
                    if t >= 2:
                        dve.wait_ge(pt_done, prob_rounds(t - 1))
                    x = prob[:, t % 2, :, 0:nk]
                    m = (cmask if br == 0 else causal)[:, i:i + 1, 0:nk].to_broadcast([P, HPG, nk])
                    chain(dve.tensor_tensor(x, SCORES[:, :, 0:nk], m, ALU.add))
                    chain(dve.tensor_reduce(out=top[:, t % 2, :], in_=x, axis=AX.X, op=ALU.max))
                    dve.tensor_scalar(ntop[:, t % 2, :], top[:, t % 2, :], -1.0, None, ALU.mult).then_inc(masked, 1)
                if t >= 6 and t % 3 == 0:
                    x = t // 3 - 2
                    at_ = (slice(None), slice(HPG * (x // 2), HPG * (x // 2 + 1)), slice((x % 2) * P, (x % 2 + 1) * P))
                    dve.wait_ge(b_hi, x + 1)
                    dve.tensor_tensor(bT_lo[at_], HO.rearrange("p (f s) -> p f s", f=HPG),
                                      bT_hi[at_].bitcast(F32), ALU.subtract).then_inc(b_read, 1)
                if 2 <= t <= STEPS + 1:
                    s = t - 2
                    g, i, br = step_of(s)
                    x = 2 * g + i
                    dve.wait_ge(probs_done, s + 1)
                    c = coef[:, s % 3, :]
                    chain(dve.tensor_scalar(c, psums[:, s % 3, :], 1e-30, None, ALU.max))
                    chain(dve.reciprocal(c, c))
                    b0 = br * HEADS + g * HPG
                    if br == 0:
                        chain(dve.tensor_scalar(c, c, rowok[:, i:i + 1], None, ALU.mult))
                    chain(dve.tensor_tensor(c, c, bgate[:, i, b0:b0 + HPG], ALU.mult))
                    dve.wait_ge(heads_done, s + 1)
                    if br == 0 and x >= 2:
                        dve.wait_ge(b_t, x - 1)
                    if br:
                        dve.wait_ge(heads_read, s)
                    for k in range(HPG):
                        dst, src = head_out[:, x % 2, k * DH:(k + 1) * DH], HO[:, k * DH:(k + 1) * DH]
                        if br == 0:
                            op = dve.tensor_scalar(dst, src, c[:, k:k + 1], None, ALU.mult)
                        else:
                            op = dve.scalar_tensor_tensor(out=dst, in0=src, scalar=c[:, k:k + 1], in1=dst,
                                                          op0=ALU.mult, op1=ALU.add)
                    op.then_inc(heads_read, 1)

            def pool_branch(n, last_unit):
                p, k = USE["gp", n]
                dve.wait_ge(pair_read[p], k)
                p, _ = USE["pu", n]
                dve.wait_ge(unit_used, last_unit + 1)
                dve.tensor_tensor(merged[:, :, n * CH:(n + 1) * CH], ACC[p], gate[:, :, :], ALU.mult)\
                   .then_inc(pair_read[p], 1)

            def nsa_branch(n, last_unit):
                p, k = USE["gn", n]
                dve.wait_ge(pair_read[p], k)
                p, _ = USE["nu", n]
                dve.wait_ge(unit_used, last_unit + 1)
                dve.wait_ge(t_done, R_M + n)
                chain(dve.tensor_tensor(tok[:, :, :], ACC[p], gate[:, :, :], ALU.mult))
                dve.tensor_tensor(tok[:, :, :], tok[:, :, :], merged[:, :, n * CH:(n + 1) * CH], ALU.add)\
                   .then_inc(pair_read[p], 1)

            for n in range(ND):
                for j in range(6):
                    u = U_ATT + 6 * n + j
                    lo(u + 1)
                    if n == 0 and j == 0:
                        dve.wait_ge(pair_read[USE["in", "gates"][0]], USE["in", "gates"][1])
                    if n == 0 and j == 1:
                        turned_plain(R_IN["q3"], qT[:, HEADS - HPG:HEADS, :])
                    if n and j == 0:
                        pool_branch(n - 1, u - 1)
                    attention(u - U_ATT)
            for n in range(ND):
                for j in range(8):
                    u = U_NSA + 8 * n + j
                    lo(u + 1)
                    if j == 0:
                        if n:
                            nsa_branch(n - 1, u - 1)
                        else:
                            pool_branch(ND - 1, u - 1)
                    if n == 0 and j < 4:
                        attention(STEPS + j)
                    if j == 2 and n:
                        d = slice(CT * (n - 1), CT * n)
                        turned_lo(R_M + n - 1, mT_lo[:, d, :], mT_hi[:, d, :])

            def out_tail(n, j):
                if j == 0:
                    residual(("wo", n), U_OUT + 4 * n + 3, n, 1.0)
                if j == 1 and n == ND - 1:
                    rstd_of(2)
                if j == 2:
                    turned_lo_gain(R_H2 + n, n, R_G2)
                    if n == ND - 1:
                        rstd_end(2)

            for n in range(ND):
                for j in range(4):
                    lo(U_OUT + 4 * n + j + 1)
                    if n:
                        out_tail(n - 1, j)
                        continue
                    if j == 0:
                        nsa_branch(ND - 1, U_OUT - 1)
                    if j == 2:
                        turned_lo(R_M + ND - 1, mT_lo[:, DT - CT:DT, :], mT_hi[:, DT - CT:DT, :])
            ffn(1, lambda j: out_tail(ND - 1, j))
            residual(("down", 1, ND - 1), U_END - 1, ND - 1, 0.5)
            dve.wait_ge(gain_loaded, 16)
            chain(gain_out(ND - 1))
            rstd_of(3)
            rstd_end(3)
            dve.wait_ge(rstd_ready, 4)
            dve.tensor_scalar(h[:, 0, :], h[:, 0, :], rstd[:, 0:1], None, ALU.mult).then_inc(unit_split, 1)

        @block.tensor
        def _(pe):
            def three(dst, xh, xl, wh, wl, start, stop):
                pe.matmul(dst, xh, wh, start=start, stop=False)
                pe.matmul(dst, xh, wl, start=False, stop=False)
                return pe.matmul(dst, xl, wh, start=False, stop=stop)

            def wait_free(key, i=None):
                p, n = USE[key]
                if n > 1:
                    pe.wait_ge(pair_read[p], by(n - 1, 1, i))

            def unit(s, key, xh, xl, k0, first, last, i=None, between=None):
                q, n = SHAPE[s]
                _, wh, wl = cols(s, q, n)
                pe.wait_ge(unit_split, by(s + 1, 8, i))
                if first:
                    wait_free(key, i)
                acc = ACC[USE[key][0]]
                for k in range(q):
                    if between is not None and k == q // 2:
                        between()
                    for m in range(HALVES):
                        x = (slice(None), k0 + k, slice(m * P, (m + 1) * P))
                        op = three(acc[:, m, 0:n], xh[x], xl[x], wh[:, k, :], wl[:, k, :],
                                   first and k == 0, last and k == q - 1)
                op.then_inc(unit_used, 1)

            def turn(r, src, i=None):
                t = T_of(r)
                if r >= ND:
                    pe.wait_ge(t_read, by(r, 1, i))
                elif r >= 2:
                    pe.wait_ge(t_read, r - 1)
                for f in range(CT):
                    for m in range(HALVES):
                        op = pe.transpose(t[:, f, m * P:(m + 1) * P], src(m, f), ident)
                op.then_inc(t_done, 1)

            def of_tok(m, f):
                return tok[:, m, f * P:(f + 1) * P]

            def of_h(n):
                return lambda m, f: h[:, m, n * CH + f * P:n * CH + (f + 1) * P]

            def wait_read(key, i=None):
                p, n = USE[key]
                pe.wait_ge(pair_read[p], by(n, 1, i))

            def wait_x(r):
                pe.wait_ge(t_read, r + 1)

            def ffn(k, r_x, tail):
                _, up, down, r0 = FFNS[k]
                for j in range(8):
                    if j < 4:
                        wait_x(r_x + j)
                    unit(up + j, (("gate", "up")[j // 4], k, 0), xT_hi, xT_lo, 4 * (j % 4), j % 4 == 0, j % 4 == 3)
                    tail(j)
                with pe.Fori(0, NFF - 1) as i:
                    for j in range(8):
                        unit(up + 8 + j, (("gate", "up")[j // 4], k, 1), xT_hi, xT_lo, 4 * (j % 4),
                             j % 4 == 0, j % 4 == 3, i)
                        if j == 1:
                            wait_read(("up", k, 0), i)
                            turn(r0, of_tok, i)
                for n in range(ND):
                    for j in range(12):
                        if n == 0 and j == 9:
                            wait_x(r0 + NFF - 1)
                        elif n == 0 and j == 0:
                            wait_x(r0 + NFF - 2)
                        unit(down + 12 * n + j, ("down", k, n), hidT_hi, hidT_lo, DOWN_K0[j], j == 0, j == 11)
                        if n:
                            down_tail(k, n - 1, j)
                        elif j == 1:
                            wait_read(("up", k, NFF - 1))
                            turn(r0 + NFF - 1, of_tok)

            def down_tail(k, n, j):
                if j == 1 and k == 0:
                    wait_read(("down", k, n))
                    turn(R_H1 + n, of_h(n))

            pe.wait_ge(const_loaded, 16)
            pe.wait_ge(small_loaded, 16 * 8)
            pe.transpose(CMP2[:, 0:P], small[:, :], ident).then_inc(small_t, 1)
            pe.wait_ge(small_ready, 1)
            for n in range(ND):
                pe.wait_ge(x_loaded[n], 16)
                turn(R_X + n, of_h(n))
            ffn(0, R_X, lambda j: None)

            def turn_piece(name):
                wait_read(("in", name))
                turn(R_IN[name], of_tok)

            for m, name in enumerate(PIECES):
                s = U_IN + START[name]
                for j in range(1 if name == "gates" else 4):
                    u = START[name] + j
                    if m == 0:
                        wait_x(R_H1 + j)
                    if name == "gates":
                        unit(s, ("in", name), xT_hi, xT_lo, 0, True, True)
                    elif name.startswith("cmp"):
                        k = int(name == "cmpv")
                        _, wh, wl = cols(s + j, 8, CMP_HIDDEN)
                        pe.wait_ge(unit_split, s + j + 1)
                        if j == 0:
                            pe.wait_ge(flat_ready, k + 1)
                        for q in range(8):
                            c = (8 * j + q) * CB
                            op = three(CMP[:, 0:CMP_HIDDEN], flat_hi[:, c:c + P], flat_lo[:, c:c + P],
                                       wh[:, q, :], wl[:, q, :], j == 0 and q == 0, j == 3 and q == 7)
                        op.then_inc(unit_used, 1)
                    else:
                        unit(s + j, ("in", name), xT_hi, xT_lo, 4 * j, j == 0, j == 3)
                    if m == 0:
                        down_tail(0, ND - 1, j)
                    elif j == 1 and PIECES[m - 1] in R_IN:
                        turn_piece(PIECES[m - 1])
                    if u in (START["cmpk"] + 5, START["cmpv"] + 5):
                        k = int(u > START["cmpk"] + 5)
                        pe.wait_ge(cmp_act, k + 1)
                        for q in range(2):
                            op = pe.transpose(CMP2[:, q * P:(q + 1) * P], cmp_h[:, q * P:(q + 1) * P], ident)
                        op.then_inc(cmp_mm, 1)
                    if u in (START["cmpk"] + 6, START["cmpv"] + 6):
                        k = int(u > START["cmpk"] + 6)
                        pe.wait_ge(cmp_copied, 2 * k + 1)
                        if k:
                            for g in range(GROUPS):
                                for q in range(2):
                                    op = pe.matmul(CMP[0:NCMP, g * DH:(g + 1) * DH],
                                                   cmp_hT[:, q, g * NCMP:(g + 1) * NCMP], cmp_w2[:, 1, q, :],
                                                   start=q == 0, stop=q == 1)
                        else:
                            for q in range(2):
                                op = pe.matmul(CMP[:, 0:CB], cmp_w2[:, 0, q, :], cmp_hT[:, q, 0:CB],
                                               start=q == 0, stop=q == 1)
                        op.then_inc(cmp_mm, 1)
                    if u in (START["p1"] + 6, START["p1"] + 8):
                        b = (u - START["p1"] - 6) // 2
                        if b == 0:
                            pe.wait_ge(pool_loaded, 32)
                            wait_read(("in", "p0"))
                            wait_read(("in", "p1"))
                            pe.wait_ge(cmp_copied, 4)
                        else:
                            pe.wait_ge(pool_read, b)
                        for f in range(CT):
                            x = 4 * b + f
                            for t in range(HALVES):
                                op = pe.matmul(T67[:, f, :], xp[:, t, x * P:(x + 1) * P], band[:, t, x // 2, :],
                                               start=t == 0, stop=t == 1)
                        op.then_inc(pool_mm, 1)
                    if u in (START["p1"] + 10, START["p1"] + 12):
                        b = (u - START["p1"] - 10) // 2
                        pe.wait_ge(pool_read, b + 2)
                        for f in range(CT):
                            x = 4 * b + f
                            for q in range(2):
                                op = pe.matmul(T67[:, f, :], pool_w[:, x // 2, q, (x % 2) * P:(x % 2 + 1) * P],
                                               pooledT[:, 2 * (x // 2) + q, :], start=q == 0, stop=q == 1)
                        op.then_inc(pool_mm, 1)

            keys = {1: ksT, 2: kwT}
            values = {1: vs, 2: vw}

            def turn_probs(x, kb):
                r = prob_rounds(x) + kb
                if kb == 0:
                    pe.wait_ge(probs_done, x + 1)
                if r:
                    pe.wait_ge(pt_copied, r)
                for k in range(HPG):
                    op = pe.transpose(PT[:, k * P:(k + 1) * P], prob[:, x % 2, k, kb * P:(kb + 1) * P], ident)
                op.then_inc(pt_done, 1)

            def attention_mid(t):
                if t < STEPS:
                    g, i, br = step_of(t)
                    nk = keys_of(t)
                    if t:
                        pe.wait_ge(masked, t)
                    for k in range(HPG):
                        q = qT[:, HPG * g + k, i * P:(i + 1) * P]
                        rhs = kcmpT[:, g * NCMP:(g + 1) * NCMP] if br == 0 else keys[br][:, g, 0:nk]
                        op = pe.matmul(SCORES[:, k, 0:nk], q, rhs, start=True, stop=True)
                    op.then_inc(scores_done, 1)
                if 1 <= t <= STEPS:
                    if t == 1:
                        wait_x(R_IN["q3"])
                    turn_probs(t - 1, 0)
                if t >= 6 and t % 3 == 0:
                    x = t // 3 - 2
                    pe.wait_ge(heads_read, 3 * x + 3)
                    pe.wait_ge(heads_read, min(t - 2, STEPS))
                    for k in range(HPG):
                        op = pe.transpose(HO[:, k * P:(k + 1) * P], head_out[:, x % 2, k * P:(k + 1) * P], ident)
                    op.then_inc(b_t, 1)

            def attention_end(t):
                if 1 <= t <= STEPS and key_tiles(t - 1) == 2:
                    turn_probs(t - 1, 1)
                if 2 <= t <= STEPS + 1:
                    s = t - 2
                    g, i, br = step_of(s)
                    n = key_tiles(s)
                    pe.wait_ge(pt_copied, prob_rounds(s) + n)
                    if s:
                        pe.wait_ge(heads_read, s)
                    if t >= 6:
                        pe.wait_ge(b_read, min(t // 3 - 1, 8))
                    for k in range(HPG):
                        for kb in range(n):
                            if br == 0:
                                w, v = probT[0:NCMP, s % 2, 0, k * P:(k + 1) * P], vcmp[0:NCMP, g, :]
                            else:
                                w = probT[:, s % 2, kb, k * P:(k + 1) * P]
                                v = values[br][:, kb, g * DH:(g + 1) * DH]
                            op = pe.matmul(HO[:, k * DH:(k + 1) * DH], w, v, start=kb == 0, stop=kb == n - 1)
                    op.then_inc(heads_done, 1)

            for n in range(ND):
                for j in range(6):
                    u = U_ATT + 6 * n + j
                    t = u - U_ATT
                    if t == 0:
                        pe.wait_ge(pool_read, 4)
                        wait_x(R_IN["q2"])
                    if j < 4:
                        unit(u, ("gp", n), xT_hi, xT_lo, 4 * j, j == 0, j == 3, between=lambda: attention_mid(t))
                    else:
                        unit(u, ("pu", n), aT_hi, aT_lo, 4 * (j - 4), j == 4, j == 5,
                             between=lambda: attention_mid(t))
                    if t == 0:
                        turn_piece("q3")
                    attention_end(t)
            for n in range(ND):
                for j in range(8):
                    u = U_NSA + 8 * n + j
                    t = u - U_ATT
                    if j < 4:
                        unit(u, ("gn", n), xT_hi, xT_lo, 4 * j, j == 0, j == 3,
                             between=(lambda: attention_mid(t)) if n == 0 else None)
                    else:
                        if n == 0 and j == 4:
                            pe.wait_ge(b_read, 8)
                        unit(u, ("nu", n), bT_hi, bT_lo, 4 * (j - 4), j == 4, j == 7)
                    if n == 0 and j < 4:
                        attention_end(t)
                    if n and j == 1:
                        wait_read(("nu", n - 1))
                        turn(R_M + n - 1, of_tok)
            for n in range(ND):
                for j in range(4):
                    if n == 0:
                        wait_x(R_M + j)
                    unit(U_OUT + 4 * n + j, ("wo", n), mT_hi, mT_lo, 4 * j, j == 0, j == 3)
                    if j == 1:
                        if n:
                            wait_read(("wo", n - 1))
                            turn(R_H2 + n - 1, of_h(n - 1))
                        else:
                            wait_read(("nu", ND - 1))
                            turn(R_M + ND - 1, of_tok)

            def out_tail(j):
                if j == 1:
                    wait_read(("wo", ND - 1))
                    turn(R_H2 + ND - 1, of_h(ND - 1))

            ffn(1, R_H2, out_tail)


def shape_tables():
    t = np.arange(S)
    c = np.zeros((P, C_END), np.float32)
    c[:, C_ID:C_ID + P] = np.eye(P, dtype=np.float32)
    for i in range(HALVES):
        tok = i * P + np.arange(P)
        c[:, C_CAUSAL + i * S:C_CAUSAL + (i + 1) * S] = np.where(t[None, :] <= tok[:, None], 0.0, NEG)
        end = np.arange(NCMP) * CMP_STRIDE + CMP_BLOCK - 1
        c[:, C_CMP + 16 * i:C_CMP + 16 * i + NCMP] = np.where(end[None, :] <= tok[:, None], 0.0, NEG)
        c[:, C_ROW + i] = tok >= CMP_BLOCK - 1
    band = np.zeros((P, HALVES, 4, S), np.float32)
    for g, win in enumerate(POOL_WINDOWS):
        inside = (t[:, None] <= t[None, :]) & (t[:, None] > t[None, :] - win)
        m = inside / np.minimum(t + 1, win)[None, :] - np.eye(S)
        band[:, :, g, :] = m.reshape(HALVES, P, S).transpose(1, 0, 2)
    return c, band


_INS = ["x", "ffn1_norm", "ffn1_w_gate", "ffn1_w_up", "ffn1_w_down", "mix_norm", "w_in", "pool_w", "pool_scale",
        "cmp_pe_k", "cmp_pe_v", "cmp_k_w1", "cmp_k_w2", "cmp_v_w1", "cmp_v_w2", "w_pool_up", "w_nsa_up", "w_out",
        "ffn2_norm", "ffn2_w_gate", "ffn2_w_up", "ffn2_w_down", "final_norm"]


def kernel(**inputs):
    import concourse.bacc as _bacc
    from concourse.bass_utils import run_bass_kernel_spmd as _run

    nc = _bacc.Bacc("TRN2", target_bir_lowering=False, num_devices=1, dynamic_dma_scratch_size=1024)
    arrays, aps = {}, {}

    def give(name, v):
        arrays[f"in_{name}"] = v
        aps[name] = nc.dram_tensor(f"in_{name}", v.shape, F32, kind="ExternalInput").ap()

    for name in _INS:
        v = np.ascontiguousarray(inputs[name])
        give(name, v if name == "final_norm" else v[0])
    consts, band = shape_tables()
    give("shape_consts", consts)
    give("pool_band", band)
    out = nc.dram_tensor("out", (S, D), F32, kind="ExternalOutput").ap()
    build_block(nc, aps, out)
    r = _run(nc, [arrays], core_ids=[0])
    return r.results[0]["out"].reshape(1, S, D)
```

```python
import numpy as np
import concourse.bass as bass
from concourse import mybir

F32 = mybir.dt.float32
F32R = mybir.dt.float32r
ALU = mybir.AluOpType
ACT = mybir.ActivationFunctionType
AX = mybir.AxisListType

P = 128
S = 256
HALVES = S // P
D = 2048
DT = D // P
FF = 5632
FT = FF // P
CH = 512
CT = CH // P
NFF = FF // CH
ND = D // CH
HEADS, GROUPS, HPG, DH = 16, 4, 4, 128
KV = GROUPS * DH
POOL_W = 1024
POOL_WINDOWS = (2, 4, 8, 16)
CMP_BLOCK, CMP_STRIDE, CMP_HIDDEN = 32, 16, 256
NCMP = S // CMP_STRIDE - 1
CB = GROUPS * NCMP
GATES = 48
EPS = 1e-6
NEG = -3.0e38
QSCALE = float(DH) ** -0.5

COL = {"p0": 0, "p1": CH, "q0": POOL_W, "q1": POOL_W + CH, "q2": POOL_W + 2 * CH, "q3": POOL_W + 3 * CH}
for _n, _name in enumerate(("kc", "vc", "ks", "vs", "kw", "vw")):
    COL[_name] = POOL_W + HEADS * DH + _n * KV
WIDE = (KV + GATES) // 2
COL["vwa"], COL["vwb"] = COL["vw"], COL["vw"] + WIDE
COL_GP = COL["vw"] + KV + GATES
COL_GN = COL_GP + D

PIECES = ["kc", "vc", "ks", "cmpk", "kw", "cmpv", "vs", "vwa", "vwb", "p0", "p1", "q0", "q1", "q2", "q3"]
START = {name: 4 * n for n, name in enumerate(PIECES)}

U_UP1 = 0
U_DOWN1 = U_UP1 + 8 * NFF
U_IN = U_DOWN1 + NFF * ND
U_ATT = U_IN + 4 * len(PIECES)
U_NSA = U_ATT + 6 * ND
U_OUT = U_NSA + 8 * ND
U_UP2 = U_OUT + 4 * ND
U_DOWN2 = U_UP2 + 8 * NFF
U_END = U_DOWN2 + NFF * ND
USE = {}


def _number_uses():
    count = {"A": 0, "B": 0}

    def use(key, pair):
        count[pair] += 1
        USE[key] = (pair, count[pair])

    for c in range(NFF):
        use(("gate", 0, c), "B")
        use(("up", 0, c), "A")
    for n in range(ND):
        use(("down", 0, n), "BA"[n % 2])
    for n, name in enumerate(x for x in PIECES if not x.startswith("cmp")):
        use(("in", name), "BA"[n % 2])
    for n in range(ND):
        use(("gp", n), "A")
        use(("pu", n), "B")
    for n in range(ND):
        use(("gn", n), "A")
        use(("nu", n), "B")
    for n in range(ND):
        use(("wo", n), "AB"[n % 2])
    for c in range(NFF):
        use(("gate", 1, c), "A")
        use(("up", 1, c), "B")
    for n in range(ND):
        use(("down", 1, n), "AB"[n % 2])


_number_uses()

R_X, R_HID1, R_H1 = 0, ND, ND + NFF
R_IN = {name: R_H1 + ND + n for n, name in enumerate(("kc", "vc", "ks", "kw", "q0", "q1", "q2", "q3"))}
R_M = R_H1 + ND + 8
R_H2 = R_M + ND
R_HID2 = R_H2 + ND
PLAIN_ROUNDS = 8


def split_no(r):
    return r + 1 if r < R_M else r + 1 - PLAIN_ROUNDS


STEPS = 6 * GROUPS


def step_of(t):
    g, j = divmod(t, 6)
    return g, j // 3, j % 3


def keys_of(t):
    _, i, br = step_of(t)
    return NCMP if br == 0 else P * (i + 1)


def key_tiles(t):
    return -(-keys_of(t) // P)


def prob_rounds(t):
    return sum(key_tiles(x) for x in range(t))


C_CAUSAL, C_CMP, C_ROW = 0, 2 * S, 2 * S + 2 * 16
C_END = C_ROW + 2
R_G1, R_GM, R_G2, R_PS, R_PEK, R_PEV = 0, DT, 2 * DT, 3 * DT, 3 * DT + 8, 3 * DT + 8 + CMP_BLOCK


def build_block(nc, a, out):
    def at(name, shape, dt, offset):
        return nc.alloc_sbuf_tensor_at(name, shape, dt, offset=offset)

    def up32(n):
        return -(-n // 32) * 32

    KB = 1024
    base = 1152
    h = at("h", [P, HALVES, D], F32, base)
    o_x = base + 16 * KB
    xT_hi = at("xT_hi", [P, DT, S], F32R, o_x)
    xT_lo = at("xT_lo", [P, DT, S], F32R, o_x + 16 * KB)
    o_w = o_x + 32 * KB
    w_raw = at("w_raw", [P, 4, 2048], F32, o_w)
    w_lo = at("w_lo", [P, 4, 2048], F32R, o_w)
    w_hi = at("w_hi", [P, 4, 1024], F32R, o_w + 32 * KB)
    o_r = o_w + 48 * KB
    hidT_hi = at("hidT_hi", [P, FT, S], F32R, o_r)
    hidT_lo = at("hidT_lo", [P, FT, S], F32R, o_r + 44 * KB)
    qT = at("qT", [P, HEADS, S], F32, o_r)
    ksT = at("ksT", [P, GROUPS, S], F32, o_r + 16 * KB)
    kwT = at("kwT", [P, GROUPS, S], F32, o_r + 20 * KB)
    vs = at("vs", [P, HALVES, KV], F32, o_r + 24 * KB)
    vw = at("vw", [P, HALVES, KV], F32, o_r + 28 * KB)
    bT_hi = at("bT_hi", [P, HEADS, S], F32R, o_r + 32 * KB)
    bT_lo = at("bT_lo", [P, HEADS, S], F32R, o_r + 48 * KB)
    band = at("band", [P, HALVES, 4, S], F32, o_r + 32 * KB)
    pooledT = at("pooledT", [P, 8, S], F32, o_r + 40 * KB)
    pool_w = at("pool_w_sb", [P, 4, 2, 256], F32, o_r + 48 * KB)
    xp = at("xp", [P, HALVES, POOL_W], F32, o_r + 56 * KB)
    kcT = at("kcT", [P, GROUPS, S], F32, o_r + 64 * KB)
    vcT = at("vcT", [P, GROUPS, S], F32, o_r + 68 * KB)
    flat = at("flat", [P, CMP_BLOCK, P], F32R, o_r + 72 * KB)
    aT_hi = at("aT_hi", [P, 8, S], F32R, o_r + 64 * KB)
    aT_lo = at("aT_lo", [P, 8, S], F32R, o_r + 72 * KB)
    prob = at("prob", [P, 2, HPG, S], F32, o_r + 80 * KB)
    mT_hi = at("mT_hi", [P, DT, S], F32R, o_r)
    mT_lo = at("mT_lo", [P, DT, S], F32R, o_r + 16 * KB)
    o_m = o_r + 88 * KB
    merged = at("merged", [P, HALVES, D], F32, o_m)
    cmp_h = at("cmp_h", [P, CMP_HIDDEN], F32, o_m + 1 * KB)
    cmp_hT = at("cmp_hT", [P, 2, CB], F32, o_m + 2 * KB)
    cmp_w2 = at("cmp_w2", [P, 2, 2, DH], F32, o_m + 3 * KB)
    flat_raw = at("flat_raw", [P, CMP_BLOCK, CB], F32, o_m + 6 * KB)
    cmp_sum = at("cmp_sum", [P, CB], F32, o_m + 14 * KB)
    o_p = o_m + 16 * KB
    probT = at("probT", [P, 2, 2, CH], F32, o_p)
    gain_last = at("gain_last", [P, D], F32, o_p)
    tok = at("tok", [P, HALVES, CH], F32, o_p + 8 * KB)
    head_out = at("head_out", [P, 2, CH], F32, o_p + 8 * KB)
    gate = at("gate", [P, HALVES, CH], F32, o_p + 12 * KB)
    o_c = o_p + 16 * KB
    const = at("const", [P, C_END], F32, o_c)
    o_t = o_c + up32(4 * C_END)
    small_id = at("small_id", [P, 2 * P], F32, o_t)
    small_T = at("small_T", [P, P], F32, o_t + 8 * P)
    o_s = o_t + 12 * P
    kcmpT = at("kcmpT", [P, CB], F32, o_s)
    vcmp = at("vcmp", [P, GROUPS, DH], F32, o_s + up32(4 * CB))
    o_s += up32(4 * CB) + 4 * KV
    bgate = at("bgate", [P, HALVES, GATES], F32, o_s)
    o_s += 4 * HALVES * GATES
    sumsq = at("sumsq", [P, HALVES, ND], F32, o_s)
    var = at("var", [P, HALVES], F32, o_s + 32)
    std = at("std", [P, HALVES], F32, o_s + 64)
    rstd = at("rstd", [P, HALVES], F32, o_s + 96)
    qstd = at("qstd", [P, HALVES], F32, o_s + 128)
    top = at("top", [P, 2, HPG], F32, o_s + 160)
    ntop = at("ntop", [P, 2, HPG], F32, o_s + 192)
    psums = at("psums", [P, 3, HPG], F32, o_s + 224)
    coef = at("coef", [P, 3, HPG], F32, o_s + 288)
    hrstd = at("hrstd", [P, HALVES], F32, o_s + 384)
    spare = at("spare", [P, 1], F32, o_s + 352)

    ps = nc.alloc_psum_tensor("ps", [P, 8 * CH], F32)

    def bank(b, n=1):
        return ps[:, b * CH:(b + n) * CH]

    ACC = {"A": bank(0, 2).rearrange("p (h n) -> p h n", h=2),
           "B": bank(2, 2).rearrange("p (h n) -> p h n", h=2)}
    T45 = bank(4, 2).rearrange("p (f s) -> p f s", f=CT)
    T67 = bank(6, 2).rearrange("p (f s) -> p f s", f=CT)
    SCORES = bank(6, 2).rearrange("p (h k) -> p h k", h=HPG)
    PT = bank(4)
    HO = bank(5)
    CMP = bank(6)
    CMP2 = bank(7)

    def T_of(r):
        return T67 if r < ND and r % 2 else T45

    ident = small_id[:, P:2 * P]
    causal = const[:, C_CAUSAL:C_CAUSAL + 2 * S].rearrange("p (i k) -> p i k", i=2)
    cmask = const[:, C_CMP:C_CMP + 32].rearrange("p (i k) -> p i k", i=2)
    rowok = const[:, C_ROW:C_ROW + 2]

    def sem(name):
        return nc.alloc_semaphore(name)

    raw_loaded = [sem(f"raw_loaded{n}") for n in range(4)]
    x_loaded = [sem(f"x_loaded{n}") for n in range(ND)]
    small_loaded = sem("small_loaded")
    const_loaded = sem("const_loaded")
    w2_loaded = sem("w2_loaded")
    pool_loaded = sem("pool_loaded")
    gain_loaded = sem("gain_loaded")
    out_stored = sem("out_stored")
    out_ready = sem("out_ready")
    out_ready_act = sem("out_ready_act")
    hi_ready = sem("hi_ready")
    part_split = sem("part_split")
    part_used = sem("part_used")
    pair_read = {p: sem(f"pair_read_{p}") for p in "AB"}
    t_done = sem("t_done")
    t_hi = sem("t_hi")
    t_read = sem("t_read")
    small_t = sem("small_t")
    small_ready = sem("small_ready")
    sumsq_ready = sem("sumsq_ready")
    var_ready = sem("var_ready")
    std_ready = sem("std_ready")
    rstd_ready = sem("rstd_ready")
    flat_raw_ready = sem("flat_raw_ready")
    flat_hi_ready = sem("flat_hi_ready")
    flat_ready = sem("flat_ready")
    cmp_act = sem("cmp_act")
    cmp_mm = sem("cmp_mm")
    cmp_copied = sem("cmp_copied")
    pool_mm = sem("pool_mm")
    pool_hi = sem("pool_hi")
    pool_read = sem("pool_read")
    scores_done = sem("scores_done")
    masked = sem("masked")
    probs_done = sem("probs_done")
    pt_done = sem("pt_done")
    pt_copied = sem("pt_copied")
    heads_done = sem("heads_done")
    heads_read = sem("heads_read")
    b_t = sem("b_t")
    b_hi = sem("b_hi")
    b_read = sem("b_read")
    dve_step = sem("dve_step")

    def by(value, step, i):
        return value if i is None else i * step + value

    def loaded(s):
        q, n = SHAPE[s]
        return w_raw[:, s % 4, 0:q * n].rearrange("p (q n) -> p q n", q=q)

    def part(s, p):
        q, n = SHAPE[s]
        m = q * n // 2
        flat = slice(p * m, (p + 1) * m)
        return w_raw[:, s % 4, flat], w_hi[:, (2 * s + p) % 4, 0:m], w_lo[:, s % 4, flat]

    def part_tiles(s, p):
        q, _ = SHAPE[s]
        _, wh, wl = part(s, p)
        return tuple(x.rearrange("p (q n) -> p q n", q=q // 2) for x in (wh, wl))

    SHAPE = {s: (4, CH) for s in range(U_END)}
    for name in ("cmpk", "cmpv", "vwa", "vwb"):
        for j in range(4):
            SHAPE[U_IN + START[name] + j] = (8, CMP_HIDDEN) if name[0] == "c" else (4, WIDE)

    FFNS = [(0, U_UP1, U_DOWN1, R_HID1), (1, U_UP2, U_DOWN2, R_HID2)]

    with nc.Block() as block:

        @block.sync
        def _(sp):
            def load(s, src, i=None):
                if s >= 4:
                    sp.wait_ge(part_used, by(2 * (s - 3), 16, i))
                sp.dma_start(loaded(s), src).then_inc(raw_loaded[s % 4], 16)

            def rows(w, k0, q, n0, n=CH):
                return w[k0 * P:(k0 + q) * P, n0:n0 + n].rearrange("(q p) n -> p q n", p=P)

            def gate_up(first, wg, wu, i=None):
                for j in range(8):
                    w = wg if j < 4 else wu
                    k = w[(j % 4) * CH:(j % 4 + 1) * CH, :].rearrange("(q p) n -> p q n", p=P)
                    src = k[:, :, 0:CH] if i is None else k[:, :, bass.ds((i + 1) * CH, CH)]
                    load(first + j, src, i)

            def ffn(k, wg, wu, wd):
                _, up, down, _ = FFNS[k]
                if k == 1:
                    gate_up(up, wg, wu)
                with sp.Fori(0, NFF - 1) as i:
                    gate_up(up + 8, wg, wu, i)
                for n in range(ND):
                    for j in range(NFF):
                        load(down + NFF * n + j, rows(wd, 4 * j, 4, n * CH))

            xv = a["x"].rearrange("(i p) d -> p i d", p=P)

            def load_x(n):
                sp.dma_start(h[:, :, n * CH:(n + 1) * CH], xv[:, :, n * CH:(n + 1) * CH]).then_inc(x_loaded[n], 16)

            sp.dma_start(small_id[:, :], a["small_params"]).then_inc(small_loaded, 16)
            wg, wu = a["ffn1_w_gate"], a["ffn1_w_up"]
            for j in range(4):
                load_x(j)
                load(j, rows(wg, 4 * j, 4, 0))
            sp.dma_start(const[:, :], a["shape_consts"][:, 0:C_END]).then_inc(const_loaded, 16)
            sp.dma_start(cmp_sum[:, :], a["shape_consts"][:, C_END:C_END + CB]).then_inc(w2_loaded, 16)
            for n, name in enumerate(("cmp_k_w2", "cmp_v_w2")):
                sp.dma_start(cmp_w2[:, n, :, :], a[name].rearrange("(q p) d -> p q d", p=P)).then_inc(w2_loaded, 16)
            for j in range(4):
                load(4 + j, rows(wu, 4 * j, 4, 0))
            ffn(0, wg, wu, a["ffn1_w_down"])

            for name in PIECES:
                s = U_IN + START[name]
                if name.startswith("cmp"):
                    w1 = a["cmp_k_w1"] if name == "cmpk" else a["cmp_v_w1"]
                    for j in range(4):
                        load(s + j, rows(w1, 8 * j, 8, 0, CMP_HIDDEN))
                else:
                    for j in range(4):
                        load(s + j, rows(a["w_in"], 4 * j, 4, COL[name], SHAPE[s][1]))
                if name == "vc":
                    sp.dma_start(band[:, :, :, :], a["pool_band"]).then_inc(pool_loaded, 16)
                    sp.dma_start(pool_w[:, :, :, :],
                                 a["pool_w"].rearrange("g (q p) d -> p g q d", p=P)).then_inc(pool_loaded, 16)
            for n in range(ND):
                for j in range(4):
                    load(U_ATT + 6 * n + j, rows(a["w_in"], 4 * j, 4, COL_GP + n * CH))
                for j in range(2):
                    load(U_ATT + 6 * n + 4 + j, rows(a["w_pool_up"], 4 * j, 4, n * CH))
            for n in range(ND):
                for j in range(4):
                    load(U_NSA + 8 * n + j, rows(a["w_in"], 4 * j, 4, COL_GN + n * CH))
                for j in range(4):
                    load(U_NSA + 8 * n + 4 + j, rows(a["w_nsa_up"], 4 * j, 4, n * CH))
            for n in range(ND):
                for j in range(4):
                    load(U_OUT + 4 * n + j, rows(a["w_out"], 4 * j, 4, n * CH))
            sp.dma_start(gain_last[:, :], a["final_norm"].partition_broadcast(P)).then_inc(gain_loaded, 16)
            ffn(1, a["ffn2_w_gate"], a["ffn2_w_up"], a["ffn2_w_down"])
            ov = out.rearrange("(i p) d -> p i d", p=P)
            sp.wait_ge(out_ready, 1)
            sp.dma_start(ov[:, 0, 0:D - CH], h[:, 0, 0:D - CH]).then_inc(out_stored, 16)
            sp.wait_ge(out_ready, 2)
            sp.dma_start(ov[:, :, D - CH:D], h[:, :, D - CH:D]).then_inc(out_stored, 16)
            sp.wait_ge(out_stored, 48)

        @block.scalar
        def _(act):
            def hi(s, i=None):
                if s >= U_END:
                    return
                act.wait_ge(raw_loaded[s % 4], by(16 * (s // 4 + 1), 32, i))
                for p in range(2):
                    if s >= 2:
                        act.wait_ge(part_used, by(2 * s + p - 3, 16, i))
                    raw, wh, _ = part(s, p)
                    act.activation(wh, raw, ACT.Copy).then_inc(hi_ready, 1)

            def wait_read(key, i=None):
                p, n = USE[key]
                act.wait_ge(pair_read[p], by(n, 1, i))

            def evacuate(key, last_unit, dst, func, scale, i=None, width=CH):
                p, _ = USE[key]
                act.wait_ge(part_used, by(2 * (last_unit + 1), 16, i))
                act.activation(dst(0), ACC[p][:, 0, 0:width], func, scale=scale[:, 0:1])
                act.activation(dst(1), ACC[p][:, 1, 0:width], func, scale=scale[:, 1:2]).then_inc(pair_read[p], 1)

            def turned_hi(r, dst, i=None):
                act.wait_ge(t_done, by(r + 1, 1, i))
                act.activation(dst, T_of(r), ACT.Copy).then_inc(t_hi, 1)

            def turned_hi_gain(r, dst, n, g0):
                act.wait_ge(t_done, r + 1)
                for f in range(CT):
                    c = g0 + CT * n + f
                    op = act.activation(dst[:, CT * n + f, :], T_of(r)[:, f, :], ACT.Copy, scale=small_T[:, c:c + 1])
                op.then_inc(t_hi, 1)

            squared = [0]

            def squares(n):
                if squared[0]:
                    act.wait_ge(sumsq_ready, squared[0])
                squared[0] += 1
                for k in range(HALVES):
                    op = act.activation(gate[:, k, :], h[:, k, n * CH:(n + 1) * CH], ACT.Square,
                                        accum_out=sumsq[:, k, n:n + 1])
                op.then_inc(sumsq_ready, 1)

            def root(k):
                act.wait_ge(var_ready, k + 1)
                act.activation(std[:, :], var[:, :], ACT.Sqrt).then_inc(std_ready, 1)

            def silu(k, first, i=None):
                key = ("gate", k, 0 if i is None else 1)
                up = ("up", k, 0 if i is None else 1)
                p, n = USE[up]
                if n > 1:
                    act.wait_ge(pair_read[p], by(n - 1, 1, i))
                evacuate(key, first + 3, lambda m: gate[:, m, :], ACT.Silu, rstd, i)

            def ffn(k, tail):
                _, up, down, r0 = FFNS[k]
                for j in range(8):
                    hi(up + j + 1)
                    tail(j)
                    if j == 4:
                        act.wait_ge(rstd_ready, 1 if k == 0 else 3)
                        silu(k, up)
                with act.Fori(0, NFF - 1) as i:
                    for j in range(8):
                        hi(up + 8 + j + 1, i)
                        if j == 2:
                            turned_hi(r0, hidT_hi[:, bass.ds(i * CT, CT), :], i)
                        if j == 4:
                            silu(k, up + 8, i)
                for n in range(ND):
                    for j in range(NFF):
                        hi(down + NFF * n + j + 1)
                        if n:
                            down_tail(k, n - 1, j)
                        elif j == 2:
                            turned_hi(r0 + NFF - 1, hidT_hi[:, FT - CT:FT, :])

            def down_tail(k, n, j):
                if j == 1:
                    wait_read(("down", k, n))
                    squares(n)
                if j == 2 and k == 0:
                    turned_hi_gain(R_H1 + n, xT_hi, n, R_GM)

            def input_head(j):
                if j < ND - 1:
                    turned_hi_gain(R_X + j + 1, xT_hi, j + 1, R_G1)
                if j < ND:
                    act.wait_ge(x_loaded[j], 16)
                    squares(j)
                if j == ND - 1:
                    root(0)

            act.wait_ge(small_ready, 1)
            turned_hi_gain(R_X, xT_hi, 0, R_G1)
            hi(0)
            ffn(0, input_head)

            outs = {"kc": tok, "vc": tok, "ks": tok, "kw": tok, "vs": vs, "vwa": vw, "vwb": vw, "p0": xp, "p1": xp,
                    "q0": tok, "q1": tok, "q2": tok, "q3": tok}
            for m, name in enumerate(PIECES):
                last = PIECES[m - 1] if m else None
                for j in range(4):
                    u = START[name] + j
                    hi(U_IN + u + 1)
                    if m == 0:
                        down_tail(0, ND - 1, j)
                        if j == 2:
                            root(1)
                    elif j == 0 and not last.startswith("cmp"):
                        if m == 1:
                            act.wait_ge(rstd_ready, 2)
                        dst = outs[last]
                        if dst is tok:
                            act.wait_ge(t_done, R_IN[last])
                        if last == "vwb":
                            act.wait_ge(part_used, 2 * (U_IN + u))
                            acc, w = ACC[USE["in", last][0]], KV - WIDE
                            for k in range(HALVES):
                                act.activation(vw[:, k, WIDE:KV], acc[:, k, 0:w], ACT.Copy, scale=rstd[:, k:k + 1])
                            for k in range(HALVES):
                                op = act.activation(bgate[:, k, :], acc[:, k, w:WIDE], ACT.Sigmoid,
                                                    scale=rstd[:, k:k + 1])
                            op.then_inc(pair_read[USE["in", last][0]], 1)
                        else:
                            n0 = CH if last == "p1" else 0
                            w = WIDE if last == "vwa" else CH
                            evacuate(("in", last), U_IN + u - 1, lambda k: dst[:, k, n0:n0 + w],
                                     ACT.Copy, qstd if last[0] == "q" else rstd, width=w)
                    if u in (START["ks"] + 1, START["kw"] + 1):
                        k = int(u > START["kw"])
                        act.wait_ge(flat_raw_ready, k + 1)
                        act.activation(flat[:, :, 0:CB], flat_raw[:, :, :], ACT.Copy).then_inc(flat_hi_ready, 1)
                    if u in (START["cmpk"] + 4, START["cmpv"] + 4):
                        k = int(u > START["cmpk"] + 4)
                        act.wait_ge(part_used, 2 * (U_IN + u))
                        act.activation(cmp_h[:, :], CMP[:, 0:CMP_HIDDEN], ACT.Copy).then_inc(cmp_act, 1)
                    if u in (START["cmpk"] + 6, START["cmpv"] + 6):
                        k = int(u > START["cmpk"] + 6)
                        act.wait_ge(cmp_mm, 2 * k + 1)
                        act.activation(cmp_hT[:, :, :], CMP2[:, 0:2 * CB].rearrange("p (q n) -> p q n", q=2), ACT.Silu)\
                           .then_inc(cmp_act, 1)
                    if u in (START["p1"] + 11, START["p1"] + 13):
                        b = (u - START["p1"] - 11) // 2
                        act.wait_ge(pool_mm, b + 3)
                        for f in range(CT):
                            c = R_PS + 4 * b + f
                            op = act.activation(aT_hi[:, 4 * b + f, :], T67[:, f, :], ACT.Copy,
                                                scale=small_T[:, c:c + 1])
                        op.then_inc(pool_hi, 1)

            def attention(t):
                def copy_turned(x, kb):
                    r = prob_rounds(x) + kb
                    act.wait_ge(pt_done, r + 1)
                    if x >= 2:
                        act.wait_ge(heads_done, x - 1)
                    m = NCMP if keys_of(x) == NCMP else P
                    act.activation(probT[0:m, x % 2, kb, :], PT[0:m, :], ACT.Copy).then_inc(pt_copied, 1)

                if 1 <= t <= STEPS:
                    copy_turned(t - 1, 0)
                if t >= 6 and t % 3 == 0:
                    x = t // 3 - 2
                    act.wait_ge(b_t, x + 1)
                    act.activation(bT_hi[:, HPG * (x // 2):HPG * (x // 2 + 1), (x % 2) * P:(x % 2 + 1) * P],
                                   HO.rearrange("p (f s) -> p f s", f=HPG), ACT.Copy).then_inc(b_hi, 1)
                if t < STEPS:
                    nk = keys_of(t)
                    act.wait_ge(masked, t + 1)
                    if t >= 3:
                        act.wait_ge(heads_read, t - 2)
                    for k in range(HPG):
                        op = act.activation(prob[:, t % 2, k, 0:nk], prob[:, t % 2, k, 0:nk], ACT.Exp,
                                            bias=ntop[:, t % 2, k:k + 1], accum_out=psums[:, t % 3, k:k + 1])
                    op.then_inc(probs_done, 1)
                if 1 <= t <= STEPS and key_tiles(t - 1) == 2:
                    copy_turned(t - 1, 1)

            for n in range(ND):
                for j in range(6):
                    u = U_ATT + 6 * n + j
                    hi(u + 1)
                    if n == 0 and j == 0:
                        act.wait_ge(t_done, R_IN["q3"])
                        evacuate(("in", "q3"), u - 1, lambda k: tok[:, k, :], ACT.Copy, qstd)
                    attention(u - U_ATT)
                    if j == 4:
                        if n:
                            wait_read(("pu", n - 1))
                        evacuate(("gp", n), u - 1, lambda k: gate[:, k, :], ACT.Tanh, hrstd)
            for n in range(ND):
                for j in range(8):
                    u = U_NSA + 8 * n + j
                    hi(u + 1)
                    if n == 0 and j < 4:
                        attention(STEPS + j)
                    if j == 2 and n:
                        turned_hi(R_M + n - 1, mT_hi[:, CT * (n - 1):CT * n, :])
                    if j == 4:
                        wait_read(("nu", n - 1) if n else ("pu", ND - 1))
                        evacuate(("gn", n), u - 1, lambda k: gate[:, k, :], ACT.Tanh, hrstd)

            def out_tail(n, j):
                if j == 1:
                    wait_read(("wo", n))
                    squares(n)
                if j == 2:
                    turned_hi_gain(R_H2 + n, xT_hi, n, R_G2)
                    if n == ND - 1:
                        root(2)

            for n in range(ND):
                for j in range(4):
                    hi(U_OUT + 4 * n + j + 1)
                    if n:
                        out_tail(n - 1, j)
                    elif j == 2:
                        turned_hi(R_M + ND - 1, mT_hi[:, DT - CT:DT, :])
            ffn(1, lambda j: out_tail(ND - 1, j))
            act.activation(spare[:, :], rstd[:, 0:1], ACT.Sqrt)
            wait_read(("down", 1, ND - 1))
            squares(ND - 1)
            root(3)
            act.wait_ge(rstd_ready, 4)
            act.activation(h[:, 1, 0:D - CH], h[:, 1, 0:D - CH], ACT.Copy, scale=rstd[:, 1:2]).then_inc(out_ready_act, 1)
            act.wait_ge(out_ready_act, 1)
            act.dma_start(out.rearrange("(i p) d -> p i d", p=P)[:, 1, 0:D - CH], h[:, 1, 0:D - CH])\
               .then_inc(out_stored, 16)

        @block.vector
        def _(dve):
            steps = [0]

            def chain(op):
                steps[0] += 1
                op.then_inc(dve_step, 1)
                dve.wait_ge(dve_step, steps[0])

            def lo(s, i=None):
                if s >= U_END:
                    return
                for p in range(2):
                    raw, wh, wl = part(s, p)
                    dve.wait_ge(hi_ready, by(2 * s + p + 1, 16, i))
                    dve.tensor_tensor(wl, raw, wh.bitcast(F32), ALU.subtract).then_inc(part_split, 1)

            def turned_lo(r, dst_lo, dst_hi, i=None):
                dve.wait_ge(t_hi, by(split_no(r), 1, i))
                dve.tensor_tensor(dst_lo, T_of(r), dst_hi.bitcast(F32), ALU.subtract).then_inc(t_read, 1)

            def turned_lo_gain(r, n, g0):
                dve.wait_ge(t_hi, split_no(r))
                for f in range(CT):
                    c, x = g0 + CT * n + f, CT * n + f
                    op = dve.scalar_tensor_tensor(out=xT_lo[:, x, :], in0=T_of(r)[:, f, :],
                                                  scalar=small_T[:, c:c + 1], in1=xT_hi[:, x, :].bitcast(F32),
                                                  op0=ALU.mult, op1=ALU.subtract)
                op.then_inc(t_read, 1)

            def turned_plain(r, dst):
                dve.wait_ge(t_done, r + 1)
                dve.tensor_copy(dst, T_of(r)).then_inc(t_read, 1)

            def rstd_of(k):
                dve.wait_ge(sumsq_ready, ND * (k + 1))
                chain(dve.tensor_reduce(out=var[:, :], in_=sumsq[:, :, :], axis=AX.X, op=ALU.add))
                dve.tensor_scalar(var[:, :], var[:, :], 1.0 / D, EPS, ALU.mult, ALU.add).then_inc(var_ready, 1)

            def rstd_end(k):
                dve.wait_ge(std_ready, k + 1)
                if k == 1:
                    chain(dve.reciprocal(rstd[:, :], std[:, :]))
                    dve.tensor_scalar(hrstd[:, :], rstd[:, :], 0.5, None, ALU.mult)
                    dve.tensor_scalar(qstd[:, :], rstd[:, :], QSCALE, None, ALU.mult).then_inc(rstd_ready, 1)
                else:
                    dve.reciprocal(rstd[:, :], std[:, :]).then_inc(rstd_ready, 1)

            def residual(key, last_unit, n, factor):
                p, _ = USE[key]
                dve.wait_ge(part_used, 2 * (last_unit + 1))
                for k in range(HALVES):
                    x = h[:, k, n * CH:(n + 1) * CH]
                    op = dve.scalar_tensor_tensor(out=x, in0=ACC[p][:, k, :], scalar=factor, in1=x,
                                                  op0=ALU.mult, op1=ALU.add)
                op.then_inc(pair_read[p], 1)

            def hidden(k, c, i=None):
                _, up, _, r0 = FFNS[k]
                p, n = USE["gate", k, c]
                dve.wait_ge(pair_read[p], by(n, 1, i))
                dve.wait_ge(part_used, by(2 * (up + 8 * (c + 1)), 16, i))
                dve.wait_ge(t_done, by(r0 + c, 1, i))
                p, _ = USE["up", k, c]
                for m in range(HALVES):
                    op = dve.scalar_tensor_tensor(out=tok[:, m, :], in0=ACC[p][:, m, :], scalar=rstd[:, m:m + 1],
                                                  in1=gate[:, m, :], op0=ALU.mult, op1=ALU.mult)
                op.then_inc(pair_read[p], 1)

            def ffn(k, tail):
                _, up, down, r0 = FFNS[k]
                for j in range(8):
                    lo(up + j + 1)
                    tail(j)
                with dve.Fori(0, NFF - 1) as i:
                    for j in range(8):
                        lo(up + 8 + j + 1, i)
                        if j == 0:
                            hidden(k, 0, i)
                        if j == 2:
                            d = bass.ds(i * CT, CT)
                            turned_lo(r0, hidT_lo[:, d, :], hidT_hi[:, d, :], i)
                for n in range(ND):
                    for j in range(NFF):
                        lo(down + NFF * n + j + 1)
                        if n:
                            down_tail(k, n - 1, j)
                            continue
                        if j == 0:
                            hidden(k, NFF - 1)
                        if j == 2:
                            turned_lo(r0 + NFF - 1, hidT_lo[:, FT - CT:FT, :], hidT_hi[:, FT - CT:FT, :])

            def gain_out(n):
                dve.wait_ge(sumsq_ready, 3 * ND + n + 1)
                for k in range(HALVES):
                    x = h[:, k, n * CH:(n + 1) * CH]
                    op = dve.tensor_tensor(x, x, gain_last[:, n * CH:(n + 1) * CH], ALU.mult)
                return op

            def down_tail(k, n, j):
                if j == 0:
                    residual(("down", k, n), FFNS[k][2] + NFF * (n + 1) - 1, n, 0.5)
                if j == 2 and k == 0:
                    turned_lo_gain(R_H1 + n, n, R_GM)
                if j == NFF - 1 and k == 1:
                    dve.wait_ge(gain_loaded, 16)
                    gain_out(n)

            def input_head(j):
                if j < ND - 1:
                    turned_lo_gain(R_X + j + 1, j + 1, R_G1)
                if j == ND - 1:
                    rstd_of(0)
                    rstd_end(0)

            dve.wait_ge(small_t, 1)
            dve.tensor_copy(small_T[:, :], CMP2[:, 0:P]).then_inc(small_ready, 1)
            dve.wait_ge(small_ready, 1)
            turned_lo_gain(R_X, 0, R_G1)
            lo(0)
            ffn(0, input_head)

            turned = {"kc": kcT, "vc": vcT, "ks": ksT, "kw": kwT}
            for m, name in enumerate(PIECES):
                for j in range(4):
                    u = START[name] + j
                    lo(U_IN + u + 1)
                    if m == 0:
                        down_tail(0, ND - 1, j)
                        if j == 1:
                            rstd_of(1)
                        if j == 2:
                            rstd_end(1)
                    if m and j == 2:
                        last = PIECES[m - 1]
                        if last in turned:
                            turned_plain(R_IN[last], turned[last][:, :, :])
                        elif last[0] == "q":
                            g = int(last[1])
                            turned_plain(R_IN[last], qT[:, HPG * g:HPG * (g + 1), :])
                    if u in (START["ks"], START["cmpk"] + 4):
                        k = int(u > START["ks"])
                        if k:
                            dve.wait_ge(part_used, 2 * (U_IN + START["cmpk"] + 4))
                        if k == 0:
                            dve.memset(flat[:, :, CB:P // 2].bitcast(F32), 0.0)
                            dve.memset(flat[:, :, P // 2 + CB:P].bitcast(F32), 0.0)
                        src = (vcT if k else kcT)[:, :, :].rearrange("p g (c r) -> p r g c", r=CMP_STRIDE)
                        dst = flat_raw[:, :, :].rearrange("p j (g n) -> p j g n", g=GROUPS)
                        pe0 = R_PEV if k else R_PEK
                        dve.wait_ge(t_read, R_IN["vc" if k else "kc"] + 1)
                        for s in range(2):
                            for g in range(GROUPS):
                                pe = small_T[:, pe0 + 16 * s:pe0 + 16 * (s + 1)].unsqueeze(2)
                                op = dve.tensor_tensor(dst[:, 16 * s:16 * (s + 1), g, :], src[:, :, g, s:s + NCMP],
                                                       pe.to_broadcast([P, 16, NCMP]), ALU.add)
                        op.then_inc(flat_raw_ready, 1)
                    if u in (START["ks"] + 2, START["kw"] + 2):
                        k = int(u > START["kw"])
                        dve.wait_ge(flat_hi_ready, k + 1)
                        dve.tensor_tensor(flat[:, :, P // 2:P // 2 + CB], flat_raw[:, :, :],
                                          flat[:, :, 0:CB].bitcast(F32), ALU.subtract).then_inc(flat_ready, 1)
                    if u in (START["cmpk"] + 8, START["cmpv"] + 8):
                        k = int(u > START["cmpk"] + 8)
                        dve.wait_ge(cmp_mm, 2 * k + 2)
                        if k:
                            dve.tensor_copy(vcmp[0:NCMP, :, :], CMP2[0:NCMP, :].rearrange("p (g d) -> p g d", g=GROUPS))\
                               .then_inc(cmp_copied, 1)
                        else:
                            dve.tensor_copy(kcmpT[:, :], CMP2[:, 2 * CB:3 * CB]).then_inc(cmp_copied, 1)
                    if u in (START["p1"] + 7, START["p1"] + 9):
                        b = (u - START["p1"] - 7) // 2
                        dve.wait_ge(pool_mm, b + 1)
                        dve.tensor_copy(pooledT[:, 4 * b:4 * b + 4, :], T67).then_inc(pool_read, 1)
                    if u in (START["p1"] + 11, START["p1"] + 13):
                        b = (u - START["p1"] - 11) // 2
                        dve.wait_ge(pool_hi, b + 1)
                        for f in range(CT):
                            c, x = R_PS + 4 * b + f, 4 * b + f
                            op = dve.scalar_tensor_tensor(out=aT_lo[:, x, :], in0=T67[:, f, :],
                                                          scalar=small_T[:, c:c + 1], in1=aT_hi[:, x, :].bitcast(F32),
                                                          op0=ALU.mult, op1=ALU.subtract)
                        op.then_inc(pool_read, 1)

            def attention(t):
                if t < STEPS:
                    g, i, br = step_of(t)
                    nk = keys_of(t)
                    dve.wait_ge(scores_done, t + 1)
                    if t >= 2:
                        dve.wait_ge(pt_done, prob_rounds(t - 1))
                    x = prob[:, t % 2, :, 0:nk]
                    m = (cmask if br == 0 else causal)[:, i:i + 1, 0:nk].to_broadcast([P, HPG, nk])
                    chain(dve.tensor_tensor(x, SCORES[:, :, 0:nk], m, ALU.add))
                    chain(dve.tensor_reduce(out=top[:, t % 2, :], in_=x, axis=AX.X, op=ALU.max))
                    dve.tensor_scalar(ntop[:, t % 2, :], top[:, t % 2, :], -1.0, None, ALU.mult).then_inc(masked, 1)
                if t >= 6 and t % 3 == 0:
                    x = t // 3 - 2
                    at_ = (slice(None), slice(HPG * (x // 2), HPG * (x // 2 + 1)), slice((x % 2) * P, (x % 2 + 1) * P))
                    dve.wait_ge(b_hi, x + 1)
                    dve.tensor_tensor(bT_lo[at_], HO.rearrange("p (f s) -> p f s", f=HPG),
                                      bT_hi[at_].bitcast(F32), ALU.subtract).then_inc(b_read, 1)
                if 2 <= t <= STEPS + 1:
                    s = t - 2
                    g, i, br = step_of(s)
                    x = 2 * g + i
                    dve.wait_ge(probs_done, s + 1)
                    c = coef[:, s % 3, :]
                    chain(dve.tensor_scalar(c, psums[:, s % 3, :], 1e-30, None, ALU.max))
                    chain(dve.reciprocal(c, c))
                    b0 = br * HEADS + g * HPG
                    if br == 0:
                        chain(dve.tensor_scalar(c, c, rowok[:, i:i + 1], None, ALU.mult))
                    chain(dve.tensor_tensor(c, c, bgate[:, i, b0:b0 + HPG], ALU.mult))
                    dve.wait_ge(heads_done, s + 1)
                    if br == 0 and x >= 2:
                        dve.wait_ge(b_t, x - 1)
                    if br:
                        dve.wait_ge(heads_read, s)
                    for k in range(HPG):
                        dst, src = head_out[:, x % 2, k * DH:(k + 1) * DH], HO[:, k * DH:(k + 1) * DH]
                        if br == 0:
                            op = dve.tensor_scalar(dst, src, c[:, k:k + 1], None, ALU.mult)
                        else:
                            op = dve.scalar_tensor_tensor(out=dst, in0=src, scalar=c[:, k:k + 1], in1=dst,
                                                          op0=ALU.mult, op1=ALU.add)
                    op.then_inc(heads_read, 1)

            def pool_branch(n, last_unit):
                p, k = USE["gp", n]
                dve.wait_ge(pair_read[p], k)
                p, _ = USE["pu", n]
                dve.wait_ge(part_used, 2 * (last_unit + 1))
                for k in range(HALVES):
                    op = dve.scalar_tensor_tensor(out=merged[:, k, n * CH:(n + 1) * CH], in0=gate[:, k, :], scalar=1.0,
                                                  in1=ACC[p][:, k, :], op0=ALU.add, op1=ALU.mult)
                op.then_inc(pair_read[p], 1)

            def nsa_branch(n, last_unit):
                p, k = USE["gn", n]
                dve.wait_ge(pair_read[p], k)
                p, _ = USE["nu", n]
                dve.wait_ge(part_used, 2 * (last_unit + 1))
                dve.wait_ge(t_done, R_M + n)
                for k in range(HALVES):
                    op = dve.scalar_tensor_tensor(out=tok[:, k, :], in0=gate[:, k, :], scalar=1.0,
                                                  in1=ACC[p][:, k, :], op0=ALU.add, op1=ALU.mult)
                chain(op)
                dve.tensor_tensor(tok[:, :, :], tok[:, :, :], merged[:, :, n * CH:(n + 1) * CH], ALU.add)\
                   .then_inc(pair_read[p], 1)

            for n in range(ND):
                for j in range(6):
                    u = U_ATT + 6 * n + j
                    lo(u + 1)
                    if n == 0 and j == 0:
                        dve.wait_ge(pair_read[USE["in", "vwb"][0]], USE["in", "vwb"][1])
                        dve.wait_ge(const_loaded, 16)
                    if n == 0 and j == 2:
                        turned_plain(R_IN["q3"], qT[:, HEADS - HPG:HEADS, :])
                    if n and j == 0:
                        pool_branch(n - 1, u - 1)
                    attention(u - U_ATT)
            for n in range(ND):
                for j in range(8):
                    u = U_NSA + 8 * n + j
                    lo(u + 1)
                    if j == 0:
                        if n:
                            nsa_branch(n - 1, u - 1)
                        else:
                            pool_branch(ND - 1, u - 1)
                    if n == 0 and j < 4:
                        attention(STEPS + j)
                    if j == 2 and n:
                        d = slice(CT * (n - 1), CT * n)
                        turned_lo(R_M + n - 1, mT_lo[:, d, :], mT_hi[:, d, :])

            def out_tail(n, j):
                if j == 0:
                    residual(("wo", n), U_OUT + 4 * n + 3, n, 0.5)
                if j == 1 and n == ND - 1:
                    rstd_of(2)
                if j == 2:
                    turned_lo_gain(R_H2 + n, n, R_G2)
                    if n == ND - 1:
                        rstd_end(2)

            for n in range(ND):
                for j in range(4):
                    lo(U_OUT + 4 * n + j + 1)
                    if n:
                        out_tail(n - 1, j)
                        continue
                    if j == 0:
                        nsa_branch(ND - 1, U_OUT - 1)
                    if j == 2:
                        turned_lo(R_M + ND - 1, mT_lo[:, DT - CT:DT, :], mT_hi[:, DT - CT:DT, :])
            ffn(1, lambda j: out_tail(ND - 1, j))
            residual(("down", 1, ND - 1), U_END - 1, ND - 1, 0.5)
            rstd_of(3)
            rstd_end(3)
            dve.wait_ge(rstd_ready, 4)
            x = h[:, 0, 0:D - CH]
            dve.tensor_scalar(x, x, rstd[:, 0:1], None, ALU.mult).then_inc(out_ready, 1)
            for k in range(HALVES):
                x = h[:, k, D - CH:D]
                op = dve.scalar_tensor_tensor(out=x, in0=x, scalar=rstd[:, k:k + 1], in1=gain_last[:, D - CH:D],
                                              op0=ALU.mult, op1=ALU.mult)
            op.then_inc(out_ready, 1)

        @block.tensor
        def _(pe):
            def three(dst, xh, xl, wh, wl, start, stop):
                pe.matmul(dst, xh, wh, start=start, stop=False)
                pe.matmul(dst, xh, wl, start=False, stop=False)
                return pe.matmul(dst, xl, wh, start=False, stop=stop)

            def wait_free(key, i=None):
                p, n = USE[key]
                if n > 1:
                    pe.wait_ge(pair_read[p], by(n - 1, 1, i))

            def unit(s, key, xh, xl, k0, first, last, i=None, between=None):
                q, n = SHAPE[s]
                acc = ACC[USE[key][0]]
                for p in range(2):
                    wh, wl = part_tiles(s, p)
                    pe.wait_ge(part_split, by(2 * s + p + 1, 16, i))
                    if first and p == 0:
                        wait_free(key, i)
                    for k in range(q // 2):
                        k1 = p * q // 2 + k
                        for m in range(HALVES):
                            x = (slice(None), k0 + k1, slice(m * P, (m + 1) * P))
                            op = three(acc[:, m, 0:n], xh[x], xl[x], wh[:, k, :], wl[:, k, :],
                                       first and k1 == 0, last and k1 == q - 1)
                    op.then_inc(part_used, 1)
                    if p == 0 and between is not None:
                        between()

            def turn(r, src, i=None):
                t = T_of(r)
                if r >= ND:
                    pe.wait_ge(t_read, by(r, 1, i))
                elif r >= 2:
                    pe.wait_ge(t_read, r - 1)
                for f in range(CT):
                    for m in range(HALVES):
                        op = pe.transpose(t[:, f, m * P:(m + 1) * P], src(m, f), ident)
                op.then_inc(t_done, 1)

            def of_tok(m, f):
                return tok[:, m, f * P:(f + 1) * P]

            def of_h(n):
                return lambda m, f: h[:, m, n * CH + f * P:n * CH + (f + 1) * P]

            def wait_read(key, i=None):
                p, n = USE[key]
                pe.wait_ge(pair_read[p], by(n, 1, i))

            def wait_x(r):
                pe.wait_ge(t_read, r + 1)

            def ffn(k, r_x, tail, within=None):
                _, up, down, r0 = FFNS[k]
                for j in range(8):
                    if j < 4:
                        wait_x(r_x + j)
                    unit(up + j, (("gate", "up")[j // 4], k, 0), xT_hi, xT_lo, 4 * (j % 4), j % 4 == 0, j % 4 == 3,
                         between=(lambda: within(j)) if within and j < ND - 1 else None)
                    tail(j)
                with pe.Fori(0, NFF - 1) as i:
                    for j in range(8):
                        unit(up + 8 + j, (("gate", "up")[j // 4], k, 1), xT_hi, xT_lo, 4 * (j % 4),
                             j % 4 == 0, j % 4 == 3, i)
                        if j == 1:
                            wait_read(("up", k, 0), i)
                            turn(r0, of_tok, i)
                for n in range(ND):
                    for j in range(NFF):
                        if n == 0 and j == NFF - 1:
                            wait_x(r0 + NFF - 1)
                        elif n == 0 and j == 0:
                            wait_x(r0 + NFF - 2)
                        unit(down + NFF * n + j, ("down", k, n), hidT_hi, hidT_lo, 4 * j, j == 0, j == NFF - 1)
                        if n:
                            down_tail(k, n - 1, j)
                        elif j == 1:
                            wait_read(("up", k, NFF - 1))
                            turn(r0 + NFF - 1, of_tok)

            def down_tail(k, n, j):
                if j == 1 and k == 0:
                    wait_read(("down", k, n))
                    turn(R_H1 + n, of_h(n))

            def turn_x(n):
                pe.wait_ge(x_loaded[n], 16)
                turn(R_X + n, of_h(n))

            pe.wait_ge(small_loaded, 16)
            pe.transpose(CMP2[:, 0:P], small_id[:, 0:P], ident).then_inc(small_t, 1)
            pe.wait_ge(small_ready, 1)
            turn_x(0)
            ffn(0, R_X, lambda j: None, lambda j: turn_x(j + 1))

            def turn_piece(name):
                wait_read(("in", name))
                turn(R_IN[name], of_tok)

            for m, name in enumerate(PIECES):
                s = U_IN + START[name]
                for j in range(4):
                    u = START[name] + j
                    if m == 0:
                        wait_x(R_H1 + j)
                    if name.startswith("cmp"):
                        k = int(name == "cmpv")
                        if j == 0:
                            pe.wait_ge(flat_ready, k + 1)
                        for p in range(2):
                            wh, wl = part_tiles(s + j, p)
                            pe.wait_ge(part_split, 2 * (s + j) + p + 1)
                            for q in range(4):
                                pos = 8 * j + 4 * p + q
                                pe.matmul(CMP[:, 0:CMP_HIDDEN], flat[:, pos, :], wh[:, q, :],
                                          start=pos == 0, stop=False)
                                op = pe.matmul(CMP[:, 0:CMP_HIDDEN], flat[:, pos, :], wl[:, q, :],
                                               start=False, stop=pos == CMP_BLOCK - 1)
                            op.then_inc(part_used, 1)
                    else:
                        unit(s + j, ("in", name), xT_hi, xT_lo, 4 * j, j == 0, j == 3)
                    if m == 0:
                        down_tail(0, ND - 1, j)
                    elif j == 1 and PIECES[m - 1] in R_IN:
                        turn_piece(PIECES[m - 1])
                    if u in (START["cmpk"] + 5, START["cmpv"] + 5):
                        k = int(u > START["cmpk"] + 5)
                        pe.wait_ge(w2_loaded, 48)
                        pe.wait_ge(cmp_act, 2 * k + 1)
                        if k:
                            pe.wait_ge(cmp_copied, 1)
                        for q in range(2):
                            op = pe.matmul(CMP2[:, q * CB:(q + 1) * CB], cmp_h[:, q * P:(q + 1) * P], cmp_sum[:, :],
                                           start=True, stop=True)
                        op.then_inc(cmp_mm, 1)
                    if u in (START["cmpk"] + 7, START["cmpv"] + 7):
                        k = int(u > START["cmpk"] + 7)
                        pe.wait_ge(cmp_act, 2 * k + 2)
                        if k:
                            for g in range(GROUPS):
                                for q in range(2):
                                    op = pe.matmul(CMP2[0:NCMP, g * DH:(g + 1) * DH],
                                                   cmp_hT[:, q, g * NCMP:(g + 1) * NCMP], cmp_w2[:, 1, q, :],
                                                   start=q == 0, stop=q == 1)
                        else:
                            for q in range(2):
                                op = pe.matmul(CMP2[:, 2 * CB:3 * CB], cmp_w2[:, 0, q, :], cmp_hT[:, q, 0:CB],
                                               start=q == 0, stop=q == 1)
                        op.then_inc(cmp_mm, 1)
                    if u in (START["p1"] + 6, START["p1"] + 8):
                        b = (u - START["p1"] - 6) // 2
                        if b == 0:
                            pe.wait_ge(pool_loaded, 32)
                            wait_read(("in", "p0"))
                            wait_read(("in", "p1"))
                            pe.wait_ge(cmp_copied, 2)
                        else:
                            pe.wait_ge(pool_read, b)
                        for f in range(CT):
                            x = 4 * b + f
                            for t in range(HALVES):
                                op = pe.matmul(T67[:, f, t * P:S], xp[:, t, x * P:(x + 1) * P],
                                               band[:, t, x // 2, t * P:S], start=t == 0, stop=t == 1)
                        op.then_inc(pool_mm, 1)
                    if u in (START["p1"] + 10, START["p1"] + 12):
                        b = (u - START["p1"] - 10) // 2
                        pe.wait_ge(pool_read, b + 2)
                        for f in range(CT):
                            x = 4 * b + f
                            for q in range(2):
                                op = pe.matmul(T67[:, f, :], pool_w[:, x // 2, q, (x % 2) * P:(x % 2 + 1) * P],
                                               pooledT[:, 2 * (x // 2) + q, :], start=q == 0, stop=q == 1)
                        op.then_inc(pool_mm, 1)

            keys = {1: ksT, 2: kwT}
            values = {1: vs, 2: vw}

            def turn_probs(x, kb):
                r = prob_rounds(x) + kb
                if kb == 0:
                    pe.wait_ge(probs_done, x + 1)
                if r:
                    pe.wait_ge(pt_copied, r)
                for k in range(HPG):
                    op = pe.transpose(PT[:, k * P:(k + 1) * P], prob[:, x % 2, k, kb * P:(kb + 1) * P], ident)
                op.then_inc(pt_done, 1)

            def attention_mid(t):
                if t < STEPS:
                    g, i, br = step_of(t)
                    nk = keys_of(t)
                    if t:
                        pe.wait_ge(masked, t)
                    for k in range(HPG):
                        q = qT[:, HPG * g + k, i * P:(i + 1) * P]
                        rhs = kcmpT[:, g * NCMP:(g + 1) * NCMP] if br == 0 else keys[br][:, g, 0:nk]
                        op = pe.matmul(SCORES[:, k, 0:nk], q, rhs, start=True, stop=True)
                    op.then_inc(scores_done, 1)
                if 1 <= t <= STEPS:
                    if t == 2:
                        wait_x(R_IN["q3"])
                    turn_probs(t - 1, 0)
                if t >= 6 and t % 3 == 0:
                    x = t // 3 - 2
                    pe.wait_ge(heads_read, 3 * x + 3)
                    pe.wait_ge(heads_read, min(t - 2, STEPS))
                    for k in range(HPG):
                        op = pe.transpose(HO[:, k * P:(k + 1) * P], head_out[:, x % 2, k * P:(k + 1) * P], ident)
                    op.then_inc(b_t, 1)

            def attention_end(t):
                if 1 <= t <= STEPS and key_tiles(t - 1) == 2:
                    turn_probs(t - 1, 1)
                if 2 <= t <= STEPS + 1:
                    s = t - 2
                    g, i, br = step_of(s)
                    n = key_tiles(s)
                    pe.wait_ge(pt_copied, prob_rounds(s) + n)
                    if s:
                        pe.wait_ge(heads_read, s)
                    if t >= 6:
                        pe.wait_ge(b_read, min(t // 3 - 1, 8))
                    for k in range(HPG):
                        for kb in range(n):
                            if br == 0:
                                w, v = probT[0:NCMP, s % 2, 0, k * P:(k + 1) * P], vcmp[0:NCMP, g, :]
                            else:
                                w = probT[:, s % 2, kb, k * P:(k + 1) * P]
                                v = values[br][:, kb, g * DH:(g + 1) * DH]
                            op = pe.matmul(HO[:, k * DH:(k + 1) * DH], w, v, start=kb == 0, stop=kb == n - 1)
                    op.then_inc(heads_done, 1)

            for n in range(ND):
                for j in range(6):
                    u = U_ATT + 6 * n + j
                    t = u - U_ATT
                    if t == 0:
                        pe.wait_ge(pool_read, 4)
                        wait_x(R_IN["q2"])
                    if j < 4:
                        unit(u, ("gp", n), xT_hi, xT_lo, 4 * j, j == 0, j == 3, between=lambda: attention_mid(t))
                    else:
                        unit(u, ("pu", n), aT_hi, aT_lo, 4 * (j - 4), j == 4, j == 5,
                             between=lambda: attention_mid(t))
                    attention_end(t)
                    if t == 1:
                        pe.wait_ge(pt_copied, 1)
                        turn_piece("q3")
            for n in range(ND):
                for j in range(8):
                    u = U_NSA + 8 * n + j
                    t = u - U_ATT
                    if j < 4:
                        unit(u, ("gn", n), xT_hi, xT_lo, 4 * j, j == 0, j == 3,
                             between=(lambda: attention_mid(t)) if n == 0 else None)
                    else:
                        if n == 0 and j == 4:
                            pe.wait_ge(b_read, 8)
                        unit(u, ("nu", n), bT_hi, bT_lo, 4 * (j - 4), j == 4, j == 7)
                    if n == 0 and j < 4:
                        attention_end(t)
                    if n and j == 1:
                        wait_read(("nu", n - 1))
                        turn(R_M + n - 1, of_tok)
            for n in range(ND):
                for j in range(4):
                    if n == 0:
                        wait_x(R_M + j)
                    unit(U_OUT + 4 * n + j, ("wo", n), mT_hi, mT_lo, 4 * j, j == 0, j == 3)
                    if j == 1:
                        if n:
                            wait_read(("wo", n - 1))
                            turn(R_H2 + n - 1, of_h(n - 1))
                        else:
                            wait_read(("nu", ND - 1))
                            turn(R_M + ND - 1, of_tok)

            def out_tail(j):
                if j == 1:
                    wait_read(("wo", ND - 1))
                    turn(R_H2 + ND - 1, of_h(ND - 1))

            ffn(1, R_H2, out_tail)


def shape_tables():
    t = np.arange(S)
    c = np.zeros((P, C_END + CB), np.float32)
    for i in range(HALVES):
        tok = i * P + np.arange(P)
        c[:, C_CAUSAL + i * S:C_CAUSAL + (i + 1) * S] = np.where(t[None, :] <= tok[:, None], 0.0, NEG)
        end = np.arange(NCMP) * CMP_STRIDE + CMP_BLOCK - 1
        c[:, C_CMP + 16 * i:C_CMP + 16 * i + NCMP] = np.where(end[None, :] <= tok[:, None], 0.0, NEG)
        c[:, C_ROW + i] = tok >= CMP_BLOCK - 1
        c[i * P // 2:i * P // 2 + CB, C_END:C_END + CB] = np.eye(CB)
    band = np.zeros((P, HALVES, 4, S), np.float32)
    for g, win in enumerate(POOL_WINDOWS):
        inside = (t[:, None] <= t[None, :]) & (t[:, None] > t[None, :] - win)
        m = inside / np.minimum(t + 1, win)[None, :] - np.eye(S)
        band[:, :, g, :] = m.reshape(HALVES, P, S).transpose(1, 0, 2)
    return c, band


_INS = ["x", "ffn1_w_gate", "ffn1_w_up", "ffn1_w_down", "w_in", "pool_w", "cmp_k_w1", "cmp_k_w2", "cmp_v_w1",
        "cmp_v_w2", "w_pool_up", "w_nsa_up", "w_out", "ffn2_w_gate", "ffn2_w_up", "ffn2_w_down", "final_norm"]


def kernel(**inputs):
    import concourse.bacc as _bacc
    from concourse.bass_utils import run_bass_kernel_spmd as _run

    nc = _bacc.Bacc("TRN2", target_bir_lowering=False, num_devices=1, dynamic_dma_scratch_size=1024)
    arrays, aps = {}, {}

    def give(name, v):
        arrays[f"in_{name}"] = v
        aps[name] = nc.dram_tensor(f"in_{name}", v.shape, F32, kind="ExternalInput").ap()

    for name in _INS:
        v = np.ascontiguousarray(inputs[name])
        give(name, v if name == "final_norm" else v[0])
    small = np.zeros((P, 2 * P), np.float32)
    small[:, P:] = np.eye(P, dtype=np.float32)
    for r, name in ((R_G1, "ffn1_norm"), (R_GM, "mix_norm"), (R_G2, "ffn2_norm"), (R_PS, "pool_scale"),
                    (R_PEK, "cmp_pe_k"), (R_PEV, "cmp_pe_v")):
        v = np.asarray(inputs[name])[0].reshape(-1, P)
        small[r:r + len(v), :P] = v
    give("small_params", small)
    consts, band = shape_tables()
    give("shape_consts", consts)
    give("pool_band", band)
    out = nc.dram_tensor("out", (S, D), F32, kind="ExternalOutput").ap()
    build_block(nc, aps, out)
    r = _run(nc, [arrays], core_ids=[0])
    return r.results[0]["out"].reshape(1, S, D)
```
